# Optimizing a Trainium2 kernel written in Bass

```python
import math
import jax, jax.numpy as jnp
from jax import lax
import numpy as np

D_MODEL = 1024
BATCH = 1
SEQ = 256
DEPTH = 1
DEC_BATCH = 8
DEC_SEQ = 4
PAST_LEN = 2048
PAGE_SIZE = 128

N_META = 16
D_HG = D_MODEL // 2
HG_HEADS = 4
HG_DK = D_HG // HG_HEADS
HG_DV = D_HG // HG_HEADS
HG_CHUNK = 16
D_SSM = D_MODEL - D_HG
SSM_GROUP = 16
SSM_GROUPS = D_SSM // SSM_GROUP
SSM_STATE = 64
D_IN = 4 * D_HG + D_SSM
PEER_HEADS = 8
PEER_NKEYS = 128
PEER_EXPERTS = PEER_NKEYS * PEER_NKEYS
PEER_TOPK = 16
PEER_DHALF = 128
PEER_BLOCK = 256
DN_ALPHA = (2.0 * DEPTH) ** 0.25
DN_BETA = (8.0 * DEPTH) ** -0.25
LN_EPS = 1e-5
RMS_EPS = 1e-6

kernel_name = 'hymba_hgrn2_s5_peer_step'

F32 = jnp.float32

def _layer_norm(x, g, b):
    mu = jnp.mean(x, axis=-1, keepdims=True)
    var = jnp.mean(jnp.square(x - mu), axis=-1, keepdims=True)
    return (x - mu) * lax.rsqrt(var + LN_EPS) * g.astype(F32) + b.astype(F32)

def _hgrn2_chunked(q, k, v, logf, s0):
    bsz, L, H, DK = q.shape
    C = HG_CHUNK if L % HG_CHUNK == 0 else L
    N = L // C

    def to_chunks(a):
        return jnp.moveaxis(a.reshape((bsz, N, C) + a.shape[2:]), 1, 0)

    mask = jnp.tril(jnp.ones((C, C), dtype=bool))[None, :, :, None, None]

    def step(S, inp):
        qc, kc, vc, lfc = inp
        bcum = jnp.cumsum(lfc, axis=1)
        rel = bcum[:, :, None] - bcum[:, None]
        decay = jnp.exp(jnp.where(mask, rel, -jnp.inf))
        att = jnp.einsum('bthk,bshk,btshk->bhts', qc, kc, decay)
        o = (jnp.einsum('bhts,bshv->bthv', att, vc)
             + jnp.einsum('bthk,bhkv->bthv', qc * jnp.exp(bcum), S))
        blast = bcum[:, -1]
        S = (jnp.exp(blast)[..., None] * S
             + jnp.einsum('bshk,bshv->bhkv', kc * jnp.exp(blast[:, None] - bcum), vc))
        return S, o

    S, o = lax.scan(step, s0, (to_chunks(q), to_chunks(k), to_chunks(v), to_chunks(logf)))
    o = jnp.moveaxis(o, 0, 1).reshape(bsz, L, H, v.shape[-1])
    return o, S

def _s5_scan(u, a_re, a_im, log_dt, b_re, b_im, c_re, c_im, d, h0_re, h0_im):
    L = u.shape[1]
    a_re = a_re.astype(F32)
    a_im = a_im.astype(F32)
    dt = jnp.exp(log_dt.astype(F32))[:, None]
    zr, zi = a_re * dt, a_im * dt
    mag = jnp.exp(zr)
    ab_re, ab_im = mag * jnp.cos(zi), mag * jnp.sin(zi)
    den = a_re * a_re + a_im * a_im
    nr = ab_re - 1.0
    coef_re = (nr * a_re + ab_im * a_im) / den
    coef_im = (ab_im * a_re - nr * a_im) / den
    b_re = b_re.astype(F32)
    b_im = b_im.astype(F32)
    bb_re = coef_re[..., None] * b_re - coef_im[..., None] * b_im
    bb_im = coef_re[..., None] * b_im + coef_im[..., None] * b_re
    bu_re = jnp.einsum('blgc,gpc->blgp', u, bb_re)
    bu_im = jnp.einsum('blgc,gpc->blgp', u, bb_im)
    a_r = jnp.broadcast_to(ab_re, bu_re.shape)
    a_i = jnp.broadcast_to(ab_im, bu_re.shape)

    def combine(e1, e2):
        a1r, a1i, b1r, b1i = e1
        a2r, a2i, b2r, b2i = e2
        return (a2r * a1r - a2i * a1i, a2r * a1i + a2i * a1r,
                a2r * b1r - a2i * b1i + b2r, a2r * b1i + a2i * b1r + b2i)

    _, _, hr, hi = lax.associative_scan(combine, (a_r, a_i, bu_re, bu_im), axis=1)
    t = jnp.arange(1, L + 1, dtype=F32)[:, None, None]
    pm = jnp.exp(zr * t)
    pr, pim = pm * jnp.cos(zi * t), pm * jnp.sin(zi * t)
    hr = hr + pr * h0_re[:, None] - pim * h0_im[:, None]
    hi = hi + pr * h0_im[:, None] + pim * h0_re[:, None]
    y = (jnp.einsum('blgp,gcp->blgc', hr, c_re.astype(F32))
         - jnp.einsum('blgp,gcp->blgc', hi, c_im.astype(F32))
         + d.astype(F32).reshape(SSM_GROUPS, SSM_GROUP) * u)
    return y, hr[:, -1], hi[:, -1]

def _peer(x2, w_q, keys, u_tab, v_tab):
    T = x2.shape[0]
    nb = -(-T // PEER_BLOCK)
    xb = jnp.pad(x2, ((0, nb * PEER_BLOCK - T), (0, 0))).reshape(nb, PEER_BLOCK, D_MODEL)
    keys = keys.astype(F32)

    def block(xt):
        q = jnp.dot(xt, w_q).reshape(PEER_BLOCK, PEER_HEADS, 2, PEER_DHALF)
        s = jnp.einsum('thcd,hcnd->thcn', q, keys)
        s1, i1 = lax.top_k(s[:, :, 0], PEER_TOPK)
        s2, i2 = lax.top_k(s[:, :, 1], PEER_TOPK)
        cand = (s1[..., :, None] + s2[..., None, :]).reshape(PEER_BLOCK, PEER_HEADS, PEER_TOPK * PEER_TOPK)
        sc, ci = lax.top_k(cand, PEER_TOPK)
        e = (jnp.take_along_axis(i1, ci // PEER_TOPK, axis=-1) * PEER_NKEYS
             + jnp.take_along_axis(i2, ci % PEER_TOPK, axis=-1))
        g = jax.nn.softmax(sc, axis=-1)
        a = jax.nn.gelu(jnp.einsum('thkd,td->thk', u_tab[e].astype(F32), xt))
        return jnp.einsum('thk,thkd->td', g * a, v_tab[e].astype(F32))

    return lax.map(block, xb).reshape(nb * PEER_BLOCK, D_MODEL)[:T]

def _layer(x, s_hg, s_re, s_im, lb, w_in, b_in, hg_norm_g, a_re, a_im, log_dt, b_re, b_im,
           c_re, c_im, d, w_glu, b_glu, w_out, ln1_g, ln1_b, pw_q, pkeys, pu, pv, ln2_g, ln2_b):
    bsz, L, _ = x.shape
    proj = jnp.einsum('bld,de->ble', x, w_in) + b_in.astype(F32)
    q = proj[..., :D_HG]
    fpre = proj[..., D_HG:2 * D_HG]
    vin = proj[..., 2 * D_HG:3 * D_HG]
    gate = proj[..., 3 * D_HG:4 * D_HG]
    u = proj[..., 4 * D_HG:]
    f = lb + (1.0 - lb) * jax.nn.sigmoid(fpre)
    logf = jnp.log(f)
    kk = (1.0 - lb) * jax.nn.sigmoid(-fpre)
    heads = lambda a: a.reshape(bsz, L, HG_HEADS, HG_DK)
    o, s_hg_new = _hgrn2_chunked(heads(q), heads(kk), vin.reshape(bsz, L, HG_HEADS, HG_DV), heads(logf), s_hg)
    o = o * lax.rsqrt(jnp.mean(o * o, axis=-1, keepdims=True) + RMS_EPS)
    o_hg = o.reshape(bsz, L, D_HG) * hg_norm_g.astype(F32) * jax.nn.silu(gate)
    y, s_re_new, s_im_new = _s5_scan(u.reshape(bsz, L, SSM_GROUPS, SSM_GROUP), a_re, a_im, log_dt,
                                     b_re, b_im, c_re, c_im, d, s_re, s_im)
    z = jax.nn.gelu(y.reshape(bsz, L, D_SSM))
    o_ssm = z * jax.nn.sigmoid(jnp.einsum('bld,de->ble', z, w_glu) + b_glu.astype(F32))
    mix = jnp.einsum('bld,de->ble', jnp.concatenate([o_hg, o_ssm], axis=-1), w_out)
    x = _layer_norm(DN_ALPHA * x + mix, ln1_g, ln1_b)
    ffn = _peer(x.reshape(bsz * L, D_MODEL), pw_q, pkeys, pu, pv).reshape(bsz, L, D_MODEL)
    x = _layer_norm(DN_ALPHA * x + ffn, ln2_g, ln2_b)
    return x, s_hg_new, s_re_new, s_im_new

def setup_inputs(seed: int = 0) -> dict:
    key = jax.random.key(seed)
    ks = jax.random.split(key, 40)
    nrm = lambda i, shape, s: s * jax.random.normal(ks[i], shape, F32)
    a_im = jnp.broadcast_to(math.pi * jnp.arange(SSM_STATE, dtype=F32), (DEPTH, SSM_GROUPS, SSM_STATE))
    return {
        'x_prompt': nrm(0, (BATCH, SEQ, D_MODEL), 1.0),
        'x_sample': nrm(1, (DEC_BATCH, DEC_SEQ, D_MODEL), 1.0),
        'state_hgrn': nrm(2, (DEPTH, DEC_BATCH, HG_HEADS, HG_DK, HG_DV), 0.5),
        'state_ssm_re': nrm(3, (DEPTH, DEC_BATCH, SSM_GROUPS, SSM_STATE), 0.5),
        'state_ssm_im': nrm(4, (DEPTH, DEC_BATCH, SSM_GROUPS, SSM_STATE), 0.5),
        'meta_tokens': nrm(5, (N_META, D_MODEL), 1.0),
        'ln_emb_g': 1.0 + nrm(6, (D_MODEL,), 0.02),
        'ln_emb_b': nrm(7, (D_MODEL,), 0.02),
        'lb_logits': nrm(8, (DEPTH + 1, D_HG), 0.1),
        'w_in': nrm(9, (DEPTH, D_MODEL, D_IN), D_MODEL ** -0.5),
        'b_in': nrm(10, (DEPTH, D_IN), 0.02),
        'hg_norm_g': 1.0 + nrm(11, (DEPTH, D_HG), 0.02),
        'ssm_a_re': -0.5 + nrm(12, (DEPTH, SSM_GROUPS, SSM_STATE), 0.01),
        'ssm_a_im': a_im + nrm(13, (DEPTH, SSM_GROUPS, SSM_STATE), 0.01),
        'ssm_log_dt': jax.random.uniform(ks[14], (DEPTH, SSM_GROUPS), F32, math.log(1e-3), math.log(1e-1)),
        'ssm_b_re': nrm(15, (DEPTH, SSM_GROUPS, SSM_STATE, SSM_GROUP), (2.0 * SSM_GROUP) ** -0.5),
        'ssm_b_im': nrm(16, (DEPTH, SSM_GROUPS, SSM_STATE, SSM_GROUP), (2.0 * SSM_GROUP) ** -0.5),
        'ssm_c_re': nrm(17, (DEPTH, SSM_GROUPS, SSM_GROUP, SSM_STATE), (2.0 * SSM_STATE) ** -0.5),
        'ssm_c_im': nrm(18, (DEPTH, SSM_GROUPS, SSM_GROUP, SSM_STATE), (2.0 * SSM_STATE) ** -0.5),
        'ssm_d': nrm(19, (DEPTH, D_SSM), 0.5),
        'w_glu': nrm(20, (DEPTH, D_SSM, D_SSM), D_SSM ** -0.5),
        'b_glu': nrm(21, (DEPTH, D_SSM), 0.02),
        'w_out': nrm(22, (DEPTH, D_MODEL, D_MODEL), DN_BETA * D_MODEL ** -0.5),
        'ln1_g': 1.0 + nrm(23, (DEPTH, D_MODEL), 0.02),
        'ln1_b': nrm(24, (DEPTH, D_MODEL), 0.02),
        'peer_w_q': nrm(25, (DEPTH, D_MODEL, PEER_HEADS * 2 * PEER_DHALF), D_MODEL ** -0.5),
        'peer_keys': nrm(26, (DEPTH, PEER_HEADS, 2, PEER_NKEYS, PEER_DHALF), PEER_DHALF ** -0.5),
        'peer_u': nrm(27, (DEPTH, PEER_EXPERTS, D_MODEL), D_MODEL ** -0.5),
        'peer_v': nrm(28, (DEPTH, PEER_EXPERTS, D_MODEL), DN_BETA),
        'ln2_g': 1.0 + nrm(29, (DEPTH, D_MODEL), 0.02),
        'ln2_b': nrm(30, (DEPTH, D_MODEL), 0.02),
    }

def reference(x_prompt, x_sample, state_hgrn, state_ssm_re, state_ssm_im, meta_tokens, ln_emb_g, ln_emb_b,
              lb_logits, w_in, b_in, hg_norm_g, ssm_a_re, ssm_a_im, ssm_log_dt, ssm_b_re, ssm_b_im,
              ssm_c_re, ssm_c_im, ssm_d, w_glu, b_glu, w_out, ln1_g, ln1_b, peer_w_q, peer_keys,
              peer_u, peer_v, ln2_g, ln2_b):
    lbs = jnp.cumsum(jax.nn.softmax(lb_logits.astype(F32), axis=0), axis=0)
    bp = x_prompt.shape[0]
    meta = jnp.broadcast_to(meta_tokens.astype(F32)[None], (bp, N_META, D_MODEL))
    xp = _layer_norm(jnp.concatenate([meta, x_prompt.astype(F32)], axis=1), ln_emb_g, ln_emb_b)
    xs = _layer_norm(x_sample.astype(F32), ln_emb_g, ln_emb_b)
    hg_p, re_p, im_p, hg_s, re_s, im_s = [], [], [], [], [], []
    for l in range(DEPTH):
        lw = (lbs[l], w_in[l], b_in[l], hg_norm_g[l], ssm_a_re[l], ssm_a_im[l], ssm_log_dt[l],
              ssm_b_re[l], ssm_b_im[l], ssm_c_re[l], ssm_c_im[l], ssm_d[l], w_glu[l], b_glu[l],
              w_out[l], ln1_g[l], ln1_b[l], peer_w_q[l], peer_keys[l], peer_u[l], peer_v[l],
              ln2_g[l], ln2_b[l])
        xp, shg, sre, sim = _layer(xp, jnp.zeros((bp, HG_HEADS, HG_DK, HG_DV), F32),
                                   jnp.zeros((bp, SSM_GROUPS, SSM_STATE), F32),
                                   jnp.zeros((bp, SSM_GROUPS, SSM_STATE), F32), *lw)
        hg_p.append(shg)
        re_p.append(sre)
        im_p.append(sim)
        xs, shg, sre, sim = _layer(xs, state_hgrn[l].astype(F32), state_ssm_re[l].astype(F32),
                                   state_ssm_im[l].astype(F32), *lw)
        hg_s.append(shg)
        re_s.append(sre)
        im_s.append(sim)
    y_prompt = xp[:, N_META:].astype(x_prompt.dtype)
    y_sample = xs.astype(x_sample.dtype)
    return (y_prompt, y_sample, jnp.stack(hg_p), jnp.stack(re_p), jnp.stack(im_p),
            jnp.stack(hg_s), jnp.stack(re_s), jnp.stack(im_s))


_drawn_inputs = setup_inputs


def setup_inputs(seed=0):
    import zlib

    import numpy as np

    out = dict(_drawn_inputs(seed))
    spreads = {}
    factors = {'hg_norm_g': 2.993, 'ssm_a_re': 18.405, 'b_glu': 23.225, 'ln2_g': 8.543, 'ln2_b': 8.083}
    for name, (base, spread) in spreads.items():
        noise = np.random.default_rng([zlib.crc32(name.encode()), seed]).standard_normal(out[name].shape)
        drawn = base * np.exp(spread * noise) if base else spread * noise
        out[name] = __import__('jax').numpy.asarray(drawn.astype(out[name].dtype))
    for name, factor in factors.items():
        out[name] = (out[name] * factor).astype(out[name].dtype)
    return out
```

```python
from contextlib import ExitStack

import concourse.bass as bass
from concourse import mybir
from concourse.alu_op_type import AluOpType as ALU

ACT = mybir.ActivationFunctionType
F32 = mybir.dt.float32
F32R = mybir.dt.float32r
U8 = mybir.dt.uint8
U32 = mybir.dt.uint32
AX = mybir.AxisListType.X

P = 128
D = 1024
DC = D // P
META, SEQ, NB, NS = 16, 256, 8, 4
NPROMPT = META + SEQ
NSAMP = NB * NS
NT = NPROMPT + NSAMP
TILES = [(0, 128), (128, 128), (256, 48)]
T2P = 16
HEADS = 4
DHG = 512
NPAIR = 16
SC = 4
NCH = NT // SC
NCP = NPROMPT // SC
PH = 8
NK = 128
TOPK = 16
NP = NT - META
ALPHA = 2.0 ** 0.25
LN_EPS = 1e-5
RMS_EPS = 1e-6
LOWEST = -3.4028234663852886e38
PI_IN = 3.1415925
TWO_PI_HI = 6.28125
TWO_PI_MID = 0.0019350051879882812
TWO_PI_LO = 3.019916050561733e-07
ROUND = 12582912.0

COLS = {}
for _name, _n in (("bq", 4), ("bf", 4), ("bu", 4), ("bglu", 4), ("lb0", 4), ("lb1", 4), ("are", 16),
                  ("aim", 16), ("ldt", 16), ("d", 16), ("h0", 2 * NPAIR * NB)):
    COLS[_name] = (sum(n for _, n in COLS.values()), _n)
NCOLS = sum(n for _, n in COLS.values())


def trunk(nc, x_prompt, x_sample, meta, state, cols_in, s5bc, rows_in, masks_in, consts_in,
          w_in, w_glu, w_out, w_q, keys_t, uv,
          y_prompt, y_sample, hg_prompt, hg_sample, ssm_out):
    ctx = ExitStack()
    with ctx:
        ARENA = 16512

        def at(name, first, shape, dt=F32):
            return nc.alloc_sbuf_tensor_at(name, shape, dt, offset=ARENA + 4 * first)

        def sem(name):
            return ctx.enter_context(nc.semaphore(name))

        bank = [ctx.enter_context(nc.psum_tensor(f"bank{i}", [P, 512], F32)) for i in range(8)]

        w_ring = at("w_ring", 0, [P, 2, DC, 512])
        x_t = at("x_t", 8192, [P, DC, NT])
        z_t = at("z_t", 8192, [P, 4, SC, NCH])
        x1_t = at("x1_t", 8192, [P, DC, NT])
        c_pow = at("c_pow", 10656, [P, 2, NPAIR, 5, 2, 16])
        v_mask = at("v_mask", 10656, [48, 9, DHG])
        q_peer = at("q_peer", 10656, [P, 2 * PH, NT])
        rows_v = at("rows_v", 15776, [P, 3, DHG])
        wglu = at("wglu", 15776, [P, 4, DHG])
        rows_emb = at("rows_emb", 17824, [P, 2, D])
        pool_tmp = at("pool_tmp", 19872, [P, 4, 256])
        v_tok = at("v_tok", 17824, [P, 3, DHG])
        gate = at("gate", 19360, [P, 3, DHG])
        keysT = at("keysT", 17824, [P, 2 * PH, NK])
        toep = at("toep", 20896, [P, NPAIR, P])
        rows_ln1 = at("rows_ln1", 20896, [P, 2, D])
        u_chan = at("u_chan", 22944, [P, 4, SC, NCH])
        z4 = at("z4", 22944, [P, NPAIR, NCH])
        ohg_t = at("ohg_t", 22944, [P, HEADS, NT])
        w1 = at("w1", 24160, [P, 2, NPAIR, SC, 2, 16])
        q_dec = at("q_dec", 24160, [P, HEADS, NT])
        k_dec = at("k_dec", 25376, [P, HEADS, NT])
        k_end = at("k_end", 26592, [P, 3, HEADS, P])
        w1c = at("w1c", 28256, [P, 2, NPAIR, SC, 16])
        pre = at("pre", 28256, [P, HEADS, NT])
        suf = at("suf", 29472, [P, HEADS, NT])
        scores = at("scores", 24160, [P, 3, 2 * PH, NK])
        s5raw = at("s5raw", 30688, [P, 4, NPAIR, 16])
        x_s5 = at("x_s5", 30688, [P, 2, NPAIR, NCH])
        h_in = at("h_in", 30688, [P, 2, NPAIR, NCH])
        o_tok = at("o_tok", 30688, [P, 3, DHG])
        o_sq = at("o_sq", 32224, [P, DHG])
        c_cmp = at("c_cmp", 33120, [P, 2, NPAIR, 5, 16])
        q_t = at("q_t", 33120, [P, HEADS, NT])
        k_t = at("k_t", 34336, [P, HEADS, NT])
        f_t = at("f_t", 35552, [P, HEADS, NT])
        x_tok = at("x_tok", 36864, [P, 3, D])
        ident = at("ident", 39936, [P, P])
        iota = at("iota", 40064, [P, P])
        mask_words = at("mask_words", 40192, [P, 252], U32)
        lane = at("lane", 40448, [P, 9])
        u4 = at("u4", 40600, [P, NPAIR, NCH])
        att = at("att", 41816, [P, 3, HEADS, P])
        du = at("du", 43352, [P, NPAIR, NCH])
        cols = at("cols", 44568, [P, NCOLS])
        fins = at("fins", 44912, [P, 2, NPAIR, 9])
        rot = at("rot", 45208, [P, 2, NPAIR, NCP])
        decay = at("decay", 47384, [P, NPAIR, NCP])
        ossm_t = at("ossm_t", 45208, [P, 4, NT])
        q_mask = at("q_mask", 46424, [P, 9, HEADS, 48])
        s_prompt = at("s_prompt", 48152, [P, HEADS, P])
        w1_t = at("w1_t", 48664, [P, 2, NPAIR, P])
        g_s5 = at("g_s5", 48664, [P, 2, NPAIR, NCP])
        s_samp = at("s_samp", 48664, [P, NB, HEADS, P])
        small = at("small", 52760, [P, 440])
        cm = at("cm", 41816, [P, 4, 256])
        cm_scan = at("cm_scan", 24160, [P, 2, NPAIR, NCP])
        gate_sig = at("gate_sig", 26592, [P, 3, DHG])

        store = at("store", 0, [P, NK, NP])
        xw = at("xw", 40192, [P, 2, DC, NP], F32R)
        raw = at("raw", 44800, [P, 4, D])
        parts = at("parts", 48896, [P, 4, 2, D // 2], F32R)
        idx_f = at("idx_f", 30688, [P, 3, 3, P])
        SPLIT = 80
        assert SPLIT * NP <= 24160
        tk_sc = at("tk_sc", 31840, [P, 3, PH, TOPK])
        tk_sum = at("tk_sum", 32224, [P, 3 * PH])
        tk_val = at("tk_val", 32256, [P, 4, TOPK])
        tk_idx = at("tk_idx", 32320, [P, 4, TOPK], U32)
        tk_idxf = at("tk_idxf", 32384, [P, 4, TOPK])
        tk_ci = at("tk_ci", 32448, [P, 2, TOPK], U32)
        tk_ab = at("tk_ab", 32480, [P, 2, 2, TOPK], U32)
        tk_abf = at("tk_abf", 32544, [P, 2, 2, TOPK])
        tk_cand = at("tk_cand", 32608, [P, 2, TOPK, TOPK])
        tk_eq = at("tk_eq", 33120, [P, 2, 2, TOPK, TOPK])
        idx_t = at("idx_t", 40192, [P, 2, NT])
        g_all = at("g_all", 40800, [P, NT])
        g_hi = at("g_hi", 41104, [P, NT], F32R)
        g_lo = at("g_lo", 41408, [P, NT])
        hot1 = at("hot1", 41712, [P, 8, P], F32R)
        hot_hi = at("hot_hi", 42736, [P, 8, P], F32R)
        hot_lo = at("hot_lo", 43760, [P, 8, P], F32R)
        w_hi = at("w_hi", 40192, [P, 2, NP], F32R)
        w_lo = at("w_lo", 40768, [P, 2, NP], F32R)
        zero = at("zero", 41344, [P, 512])
        y_t = at("y_t", 0, [P, DC, NT])
        rows_ln2 = at("rows_ln2", 2432, [P, 2, D])

        taken = [0]

        def vec(n):
            taken[0] += n
            assert taken[0] <= 440
            return small[:, taken[0] - n:taken[0]]

        def col(name):
            a, n = COLS[name]
            return cols[:, a:a + n]

        s5v = [vec(16) for _ in range(22)]
        stats = vec(36)
        mv = vec(6)
        rstd = vec(6)
        lbv = vec(24)
        rms = vec(12)

        JOBS = [("xT", t, i) for t in range(3) for i in range(2)]
        JOBS += [("u", m) for m in range(4)] + [("f", m) for m in range(4)]
        JOBS += [("w1T", b) for b in range(8)] + [("toep", b) for b in range(4)]
        JOBS += [("q", m) for m in range(4)] + [("X", b) for b in range(6)]
        JOBS += [("v", t) for t in range(3)] + [("gate", t) for t in range(3)]
        LEVELS = [0, 1, 2, 4, 8, 16, 32, 64]

        def level_tiles(h):
            return [0, 1, 2] if h <= 8 else [0, 1]

        for h in LEVELS:
            JOBS += [("att", h, t) for t in level_tiles(h)]
            if h == 0:
                JOBS += [("y", b) for b in range(3)]
        JOBS += [("kend", t) for t in range(3)]
        JOBS += [("o", 0), ("S", 0), ("o", 1), ("S", 1), ("o", 2), ("S", 2)]
        JOBS += [("Sb", b) for b in range(NB)]
        JOBS += [("glu", m) for m in range(4)] + [("oT", t) for t in range(3)]
        JOBS += [("mix", t, i) for i in range(2) for t in range(3)]
        JOBS += [("x1T", t, i) for t in range(3) for i in range(2)]
        for g in range(4):
            JOBS += [("Q", 4 * g + m) for m in range(4)] + [("sc", g, t) for t in range(3)]
        J = {name: n for n, name in enumerate(JOBS)}
        assert len(J) == len(JOBS)

        ps_full = sem("ps_full")
        ps_read = [sem(f"ps_read{i}") for i in range(8)]

        def bank_of(*name):
            return bank[J[name] % 8]

        def computed(eng, *name):
            eng.wait_ge(ps_full, J[name] + 1)

        def readout(ins, *name):
            ins.then_inc(ps_read[J[name] % 8], 1)

        def evacuated(eng, *name):
            eng.wait_ge(ps_read[J[name] % 8], J[name] // 8 + 1)

        x_in = sem("x_in")
        cols_sem = sem("cols_sem")
        rows_sem = sem("rows_sem")
        consts_sem = sem("consts_sem")
        masks_sem = sem("masks_sem")
        rowsv_sem = sem("rowsv_sem")
        w_loaded = [sem(f"w_loaded{i}") for i in range(2)]
        w_used = sem("w_used")
        u4_moved = sem("u4_moved")
        z_moved = sem("z_moved")
        wglu_sem = sem("wglu_sem")
        keys_sem = sem("keys_sem")
        rows1_sem = sem("rows1_sem")
        s0_sem = sem("s0_sem")
        out_sem = sem("out_sem")
        uv_landed = [sem(f"uv_landed{i}") for i in range(4)]
        dch, ach, pch = sem("vector_chain"), sem("scalar_chain"), sem("gpsimd_chain")
        ln_var = sem("ln_var")
        ln_std = sem("ln_std")
        x0_ready = sem("x0_ready")
        zi_ready = sem("zi_ready")
        dt_ready = sem("dt_ready")
        zr_ready = sem("zr_ready")
        mag_ready = sem("mag_ready")
        sin_arg = sem("sin_arg")
        sin_ready = sem("sin_ready")
        abar_ready = sem("abar_ready")
        lb_arg = sem("lb_arg")
        lb_exp = sem("lb_exp")
        w1_ready = sem("w1_ready")
        cpow_ready = sem("cpow_ready")
        rot_ready = sem("rot_ready")
        zeroed = sem("zeroed")
        toep_ready = sem("toep_ready")
        f_pre = sem("f_pre")
        hin_ready = sem("hin_ready")
        du_ready = sem("du_ready")
        lvl_ready = sem("lvl_ready")
        pre_done = sem("pre_done")
        gate_b = sem("gate_b")
        gate_s = sem("gate_s")
        gate_done = sem("gate_done")
        qm_ready = sem("qm_ready")
        vm_ready = sem("vm_ready")
        z_ready = sem("z_ready")
        s_ready = sem("s_ready")
        s0_scaled = sem("s0_scaled")
        sb_ready = sem("sb_ready")
        fins_ready = sem("fins_ready")
        ms_ready = sem("ms_ready")
        rms_ready = sem("rms_ready")
        og_ready = sem("og_ready")
        glu_s = sem("glu_s")
        x1_ready = sem("x1_ready")
        xw_ready = sem("xw_ready")
        tk_neg = sem("tk_neg")
        tk_exp = sem("tk_exp")
        idx_ready = sem("idx_ready")
        hi_ready = sem("hi_ready")
        lo_ready = sem("lo_ready")
        parts_used = sem("parts_used")
        gelu_done = sem("gelu_done")
        idxT_full = sem("idxT_full")
        hot_ready = sem("hot_ready")
        hot_used = sem("hot_used")
        g_used = sem("g_used")
        whi_ready = sem("whi_ready")
        wlo_ready = sem("wlo_ready")
        zero_ready = sem("zero_ready")
        yT_ready = sem("yT_ready")
        yj_full = sem("yj_full")
        yj_read = sem("yj_read")
        rows2_sem = sem("rows2_sem")
        y_out_ready = sem("y_out_ready")
        rot_start = sem("rot_start")
        decay_ready = sem("decay_ready")
        tot_used = sem("tot_used")

        def chain(eng, s):
            count = [0]

            def link(ins):
                count[0] += 1
                ins.then_inc(s, 1)
                eng.wait_ge(s, count[0])
            return link

        def cmul(eng, link, out, x, a, tmp):
            eng.tensor_tensor(tmp[0], x[0], a[0], ALU.mult)
            eng.tensor_tensor(tmp[1], x[1], a[1], ALU.mult)
            eng.tensor_tensor(tmp[2], x[0], a[1], ALU.mult)
            link(eng.tensor_tensor(tmp[3], x[1], a[0], ALU.mult))
            eng.tensor_tensor(out[0], tmp[0], tmp[1], ALU.subtract)
            link(eng.tensor_tensor(out[1], tmp[2], tmp[3], ALU.add))

        def cmul_conj(eng, link, out, x, a, tmp):
            eng.tensor_tensor(tmp[0], x[0], a[0], ALU.mult)
            eng.tensor_tensor(tmp[1], x[1], a[1], ALU.mult)
            eng.tensor_tensor(tmp[2], x[1], a[0], ALU.mult)
            link(eng.tensor_tensor(tmp[3], x[0], a[1], ALU.mult))
            eng.tensor_tensor(out[0], tmp[0], tmp[1], ALU.add)
            link(eng.tensor_tensor(out[1], tmp[2], tmp[3], ALU.subtract))

        def wide(v, n):
            return v.unsqueeze(2).broadcast_to([P, NPAIR, n])

        masks = mask_words[:, :].bitcast(U8)

        def mask(h, t):
            k = [0, 1, 2, 4, 8, 16].index(h)
            if t < 2:
                m, w, n = masks[:, k * 128:(k + 1) * 128], 128, 128
            else:
                m, w, n = masks[:48, 768 + k * 48:768 + (k + 1) * 48], 48, 48
            return m.unsqueeze(1).broadcast_to([n, HEADS, w])

        w_groups = [(w_in, 2048), (w_in, 512), (w_in, 0), (w_in, 1024), (w_in, 1536),
                    (w_out, 0), (w_out, 512), (w_q, 0), (w_q, 512), (w_q, 1024), (w_q, 1536)]
        W_LAST = [("u", 3), ("f", 3), ("q", 3), ("v", 2), ("gate", 2), ("mix", 2, 0), ("mix", 2, 1)]
        W_LAST += [("Q", 4 * g + 3) for g in range(4)]
        W_GROUP = {"u": 0, "f": 1, "q": 2, "v": 3, "gate": 4}

        (dt_, zr, zi, mag, sn, cs, ar, ai, kk_, r_, den, nr, t1, t2, cr, ci, p2r, p2i, a4r, a4i,
         m4, absr) = s5v
        a_bar = (ar, ai)

        block = ctx.enter_context(nc.Block())

        @block.sync
        def _(sp):
            sp.dma_start(x_tok[0:META, 0, :], meta).then_inc(x_in, 16)
            sp.dma_start(x_tok[META:P, 0, :], x_prompt[0:112, :]).then_inc(x_in, 16)
            sp.dma_start(x_tok[:, 1, :], x_prompt[112:240, :]).then_inc(x_in, 16)
            sp.dma_start(x_tok[0:T2P, 2, :], x_prompt[240:256, :]).then_inc(x_in, 16)
            sp.dma_start(x_tok[T2P:48, 2, :], x_sample).then_inc(x_in, 16)
            sp.dma_start(cols[:, :], cols_in).then_inc(cols_sem, 16)
            sp.dma_start(s5raw[:, :, :, :].rearrange("p a b c -> p (a b c)"), s5bc).then_inc(cols_sem, 16)
            for i in range(2):
                sp.dma_start(rows_emb[:, i, :], rows_in[i, :].partition_broadcast(P)).then_inc(rows_sem, 16)
            sp.dma_start(ident[:, :], consts_in[:, 0:P]).then_inc(consts_sem, 16)
            sp.dma_start(iota[:, :], consts_in[:, P:2 * P]).then_inc(consts_sem, 16)
            sp.dma_start(lane[:, :], consts_in[:, 2 * P:2 * P + 9]).then_inc(consts_sem, 16)

            def load_w(n):
                if n >= 2:
                    computed(sp, *W_LAST[n - 2])
                w, c0 = w_groups[n]
                sp.dma_start(w_ring[:, n % 2, :, :],
                             w[:, c0:c0 + 512].rearrange("(c p) e -> p c e", p=P)).then_inc(w_loaded[n % 2], 16)

            load_w(0)
            sp.dma_start(mask_words[:, :], masks_in).then_inc(masks_sem, 16)
            load_w(1)
            sp.dma_start(rows_v[:, 0:2, :].rearrange("p a b -> p (a b)"),
                         rows_in[2, :].partition_broadcast(P)).then_inc(rowsv_sem, 16)
            sp.dma_start(rows_v[:, 2, :], rows_in[7, 0:DHG].partition_broadcast(P)).then_inc(rowsv_sem, 16)
            for m in range(4):
                evacuated(sp, "u", m)
            for j in range(SC):
                for q in range(4):
                    sp.dma_start(u4[32 * j:32 * j + 32, :, :].rearrange("p (m q) n -> p m q n", q=4)[:, :, q, :],
                                 u_chan[32 * q:32 * q + 32, :, j, :]).then_inc(u4_moved, 16)
            for n in range(2, 7):
                load_w(n)
            sp.wait_ge(gate_done, 3)
            sp.dma_start(wglu[:, :, :], w_glu.rearrange("(c p) e -> p c e", p=P)).then_inc(wglu_sem, 16)
            sp.wait_ge(hin_ready, 1)
            for b in range(NB):
                sp.dma_start(s_samp[:, b, :, :], state[b].rearrange("h k v -> k h v")).then_inc(s0_sem, 16)
            sp.wait_ge(z_ready, 3)
            for j in range(SC):
                for q in range(4):
                    sp.dma_start(z_t[32 * q:32 * q + 32, :, j, :],
                                 z4[32 * j:32 * j + 32, :, :].rearrange("p (m q) n -> p m q n", q=4)[:, :, q, :]
                                 ).then_inc(z_moved, 16)
            computed(sp, "y", 2)
            for i in range(2):
                sp.dma_start(rows_ln1[:, i, :], rows_in[3 + i, :].partition_broadcast(P)).then_inc(rows1_sem, 16)
            computed(sp, "Sb", NB - 1)
            sp.wait_ge(og_ready, 3)
            sp.wait_ge(vm_ready, 9)
            sp.dma_start(keysT[:, :, :], keys_t).then_inc(keys_sem, 16)
            sp.wait_ge(fins_ready, 1)
            sp.dma_start(ssm_out, fins[:, :, :, :].rearrange("p a b c -> p (a b c)")).then_inc(out_sem, 16)
            evacuated(sp, "S", 2)
            sp.dma_start(hg_prompt.rearrange("h k v -> k h v"), s_prompt[:, :, :]).then_inc(out_sem, 16)
            for b in range(NB):
                evacuated(sp, "Sb", b)
                sp.dma_start(hg_sample[b].rearrange("h k v -> k h v"), s_samp[:, b, :, :]).then_inc(out_sem, 16)
            for n in range(7, 11):
                load_w(n)

            computed(sp, "mix", 2, 1)
            sp.wait_ge(out_sem, 16 * 10)
            for s in range(4):
                sp.dma_start(raw[:, s, :], uv[s]).then_inc(uv_landed[s], 16)
            with sp.Fori(0, 2 * NK // 4 - 1, 1) as i:
                for s in range(4):
                    sp.wait_ge(lo_ready, 8 * i + 2 * (s + 1))
                    sp.dma_start(raw[:, s, :], uv[bass.ds(4 * i + (s + 4), 1)].squeeze(0)
                                 ).then_inc(uv_landed[s], 16)
            sp.wait_ge(parts_used, 4 * NK + 4)
            for i in range(2):
                sp.dma_start(rows_ln2[:, i, :], rows_in[5 + i, :].partition_broadcast(P)).then_inc(rows2_sem, 16)
            sp.wait_ge(y_out_ready, 1)
            sp.dma_start(y_prompt[0:112, :], x_tok[META:P, 0, :]).then_inc(out_sem, 16)
            sp.wait_ge(y_out_ready, 2)
            sp.dma_start(y_prompt[112:240, :], x_tok[:, 1, :]).then_inc(out_sem, 16)
            sp.wait_ge(y_out_ready, 3)
            sp.dma_start(y_prompt[240:256, :], x_tok[0:T2P, 2, :]).then_inc(out_sem, 16)
            sp.dma_start(y_sample, x_tok[T2P:48, 2, :]).then_inc(out_sem, 16)
            sp.wait_ge(out_sem, 16 * 14)

        @block.tensor
        def _(pe):
            def begin(*name):
                n = J[name]
                if n >= 8:
                    pe.wait_ge(ps_read[n % 8], n // 8)
                return bank[n % 8]

            mm = nc.tensor.matmul

            def transposes(name, srcs):
                b = begin(*name)
                for k, (src, n) in enumerate(srcs):
                    last = nc.tensor.transpose(b[:, k * n:(k + 1) * n], src, ident[:n, :n])
                last.then_inc(ps_full, 1)

            def x_transposes(kind, t):
                t0, n = TILES[t]
                for i in range(2):
                    transposes((kind, t, i), [(x_tok[:n, t, (4 * i + c) * P:(4 * i + c + 1) * P], n)
                                              for c in range(4)])

            pe.wait_ge(consts_sem, 48)
            for t in range(3):
                pe.wait_ge(x0_ready, t + 1)
                x_transposes("xT", t)

            def weights(n):
                pe.wait_ge(w_loaded[n % 2], 16 * (n // 2 + 1))
                return w_ring[:, n % 2, :, :]

            def project(kind):
                w = weights(W_GROUP[kind])
                for m in range(4):
                    b = begin(kind, m)
                    for c in range(DC):
                        last = mm(b[:, 0:NT], w[:, c, m * P:(m + 1) * P], x_t[:, c, :],
                                  start=c == 0, stop=c == DC - 1)
                    last.then_inc(ps_full, 1)

            def project_tok(kind):
                w = weights(W_GROUP[kind])
                for t, (t0, n) in enumerate(TILES):
                    b = begin(kind, t)
                    for c in range(DC):
                        last = mm(b[:n, :], x_t[:, c, t0:t0 + n], w[:, c, :], start=c == 0, stop=c == DC - 1)
                    last.then_inc(ps_full, 1)

            for t in range(3):
                for i in range(2):
                    evacuated(pe, "xT", t, i)
            project("u")
            project("f")

            pe.wait_ge(w1_ready, 1)
            w1f = w1[:, :, :, :, :, :].rearrange("p r a j g c -> p (r a) (j g c)")
            for b8 in range(8):
                transposes(("w1T", b8), [(w1f[:, 4 * b8 + k, :], P) for k in range(4)])
            pe.wait_ge(cpow_ready, 1)
            cpf = c_pow[:, :, :, :, :, :].rearrange("p r a t g c -> p r a (t g c)")
            for b4 in range(4):
                b = begin("toep", b4)
                for k in range(4):
                    pair = 4 * b4 + k
                    for i in range(SC):
                        for r in range(2):
                            last = mm(b[32 * i:32 * i + 32, k * P + 32 * i:(k + 1) * P],
                                      w1f[:, r * NPAIR + pair, 96:128], cpf[:, r, pair, 0:P - 32 * i],
                                      start=r == 0, stop=r == 1, tile_position=(0, 32 * i))
                last.then_inc(ps_full, 1)

            project("q")

            for j in range(8):
                evacuated(pe, "w1T", j)
            pe.wait_ge(u4_moved, 16 * 16)
            w1tf = w1_t[:, :, :, :].rearrange("p r a s -> p (r a) s")
            for b6 in range(6):
                b = begin("X", b6)
                units = range(6 * b6, min(6 * b6 + 6, 32))
                for k, un in enumerate(units):
                    last = mm(b[:, k * NCH:(k + 1) * NCH], w1tf[:, un, :], u4[:, un % NPAIR, :],
                              start=True, stop=True)
                last.then_inc(ps_full, 1)

            project_tok("v")
            project_tok("gate")

            def levels(h):
                if h:
                    pe.wait_ge(lvl_ready, LEVELS.index(h))
                for t in level_tiles(h):
                    t0, n = TILES[t]
                    b = begin("att", h, t)
                    for hd in range(HEADS):
                        kk = k_dec if h else k_t
                        qq = q_dec if h else q_t
                        last = mm(b[:n, hd * P:hd * P + n], kk[:, hd, t0:t0 + n], qq[:, hd, t0:t0 + n],
                                  start=True, stop=True)
                    last.then_inc(ps_full, 1)

            for m in range(4):
                evacuated(pe, "q", m)
                evacuated(pe, "f", m)
            pe.wait_ge(f_pre, 4)
            levels(0)

            for i in range(4):
                evacuated(pe, "toep", i)
            pe.wait_ge(hin_ready, 1)
            for b3 in range(3):
                b = begin("y", b3)
                for k, pair in enumerate(range(6 * b3, min(6 * b3 + 6, NPAIR))):
                    o = b[:, k * NCH:(k + 1) * NCH]
                    mm(o, toep[:, pair, :], u4[:, pair, :], start=True, stop=False)
                    for r in range(2):
                        last = mm(o, cpf[:, r, pair, 32:160], h_in[:, r, pair, 0:NCH], start=False, stop=r == 1)
                last.then_inc(ps_full, 1)

            for h in LEVELS[1:]:
                levels(h)

            pe.wait_ge(pre_done, 1)
            for t, (t0, n) in enumerate(TILES):
                b = begin("kend", t)
                for hd in range(HEADS):
                    last = nc.tensor.transpose(b[:n, hd * P:(hd + 1) * P], k_dec[:, hd, t0:t0 + n], ident[:, :])
                last.then_inc(ps_full, 1)

            for t in range(3):
                evacuated(pe, "v", t)
                evacuated(pe, "kend", t)
            for h in LEVELS:
                for t in level_tiles(h):
                    evacuated(pe, "att", h, t)
            for t, (t0, n) in enumerate(TILES):
                b = begin("o", t)
                if t == 1:
                    evacuated(pe, "S", 0)
                if t == 2:
                    evacuated(pe, "S", 1)
                    pe.wait_ge(qm_ready, 1)
                    pe.wait_ge(s0_sem, 16 * NB)
                for hd in range(HEADS):
                    o = b[:n, hd * P:(hd + 1) * P]
                    last = mm(o, att[:n, t, hd, 0:n], v_tok[:n, t, hd * P:(hd + 1) * P], start=True, stop=t == 0)
                    if t == 1:
                        last = mm(o, q_dec[:, hd, t0:t0 + n], s_prompt[:, hd, :], start=False, stop=True)
                    if t == 2:
                        last = mm(o, q_mask[:, 0, hd, :], s_prompt[:, hd, :], start=False, stop=False)
                        for g in range(NB):
                            last = mm(o, q_mask[:, 1 + g, hd, :], s_samp[:, g, hd, :], start=False,
                                      stop=g == NB - 1)
                last.then_inc(ps_full, 1)
                if t == 2:
                    pe.wait_ge(vm_ready, 9)
                b = begin("S", t)
                for hd in range(HEADS):
                    vv = v_mask[:, 0, hd * P:(hd + 1) * P] if t == 2 else v_tok[:n, t, hd * P:(hd + 1) * P]
                    last = mm(b[:, hd * P:(hd + 1) * P], k_end[:n, t, hd, :], vv, start=True, stop=True)
                last.then_inc(ps_full, 1)
            for g in range(NB):
                b = begin("Sb", g)
                for hd in range(HEADS):
                    last = mm(b[:, hd * P:(hd + 1) * P], k_end[:48, 2, hd, :],
                              v_mask[:, 1 + g, hd * P:(hd + 1) * P], start=True, stop=True)
                last.then_inc(ps_full, 1)

            pe.wait_ge(z_moved, 16 * 16)
            pe.wait_ge(wglu_sem, 16)
            for m in range(4):
                b = begin("glu", m)
                for c in range(4):
                    last = mm(b[:, 0:NT], wglu[:, c, m * P:(m + 1) * P],
                              z_t[:, c, :, :].rearrange("p j n -> p (j n)"), start=c == 0, stop=c == 3)
                last.then_inc(ps_full, 1)
            for t, (t0, n) in enumerate(TILES):
                pe.wait_ge(og_ready, t + 1)
                transposes(("oT", t), [(o_tok[:n, t, hd * P:(hd + 1) * P], n) for hd in range(HEADS)])

            for i in range(2):
                w = weights(5 + i)
                for t, (t0, n) in enumerate(TILES):
                    if i == 0:
                        evacuated(pe, "oT", t)
                    if i == 0 and t == 0:
                        pe.wait_ge(glu_s, 4)
                    b = begin("mix", t, i)
                    for c in range(DC):
                        src = ohg_t[:, c, t0:t0 + n] if c < 4 else ossm_t[:, c - 4, t0:t0 + n]
                        last = mm(b[:n, :], src, w[:, c, :], start=c == 0, stop=c == DC - 1)
                    last.then_inc(ps_full, 1)
            for t in range(3):
                pe.wait_ge(x1_ready, t + 1)
                x_transposes("x1T", t)

            for t in range(3):
                for i in range(2):
                    evacuated(pe, "x1T", t, i)
            for g in range(4):
                w = weights(7 + g)
                for m in range(4):
                    b = begin("Q", 4 * g + m)
                    for c in range(DC):
                        last = mm(b[:, 0:NT], w[:, c, m * P:(m + 1) * P], x1_t[:, c, :],
                                  start=c == 0, stop=c == DC - 1)
                    last.then_inc(ps_full, 1)
                if g == 0:
                    pe.wait_ge(keys_sem, 16)
                for m in range(4):
                    evacuated(pe, "Q", 4 * g + m)
                for t, (t0, n) in enumerate(TILES):
                    b = begin("sc", g, t)
                    for m in range(4):
                        last = mm(b[:n, m * P:(m + 1) * P], q_peer[:, 4 * g + m, t0:t0 + n],
                                  keysT[:, 4 * g + m, :], start=True, stop=True)
                    last.then_inc(ps_full, 1)

            for k in range(8):
                n = max(j for j in range(len(JOBS)) if j % 8 == k)
                pe.wait_ge(ps_read[k], n // 8 + 1)
            pe.wait_ge(xw_ready, 2)
            pe.sem_inc(parts_used, 4)

            def u_blocks(i):
                for s in range(4):
                    pe.wait_ge(gelu_done, 4 * i + (s + 1))
                    for c in range(DC):
                        if c % 4 == 0:
                            pe.wait_ge(lo_ready, 8 * i + (2 * s + c // 4 + 1))
                        w = parts[:, (2 * s + c // 4) % 4, :, (c % 4) * P:(c % 4 + 1) * P]
                        for (a, x) in ((0, 0), (0, 1), (1, 0)):
                            last = mm(bank[s][:, 0:NP], w[:, a, :], xw[:, x, c, :],
                                      start=(c == 0 and (a, x) == (0, 0)), stop=(c == DC - 1 and a == 1))
                        if c % 4 == 3:
                            last.then_inc(parts_used, 1)

            with pe.Fori(0, SPLIT // 4, 1) as i:
                u_blocks(i)
            for t, (t0, n) in enumerate(TILES):
                pe.wait_ge(idx_ready, t + 1)
                for a in range(3):
                    last = nc.tensor.transpose(bank[5 + t][:, a * n:(a + 1) * n], idx_f[:n, t, a, :], ident[:n, :n])
                last.then_inc(idxT_full, 1)
            with pe.Fori(SPLIT // 4, NK // 4, 1) as i:
                u_blocks(i)
            pe.wait_ge(gelu_done, NK + 4)
            pe.sem_inc(hot_used, 8)
            with pe.Fori(0, NP // 8, 1) as i:
                for u in range(8):
                    b = bank[3 + u // 4]
                    if u % 4 == 0:
                        pe.wait_ge(g_used, 2 * i + (u // 4 + 1))
                    pe.wait_ge(hot_ready, 24 * i + 3 * (u + 1))
                    mm(b[:, (u % 4) * P:(u % 4 + 1) * P], hot1[:, u, :], hot_hi[:, u, :], start=True, stop=False)
                    mm(b[:, (u % 4) * P:(u % 4 + 1) * P], hot1[:, u, :], hot_lo[:, u, :], start=False,
                       stop=True).then_inc(hot_used, 1)

            pe.wait_ge(zero_ready, 1)
            pe.wait_ge(g_used, 2 + NP // 4)
            for k in range(8):
                mm(bank[k][:, 0:NP], zero[0:1, 0:P], zero[0:1, 0:NP], start=True, stop=False, skip_group_check=True)
            with pe.Fori(0, NK // 2, 1) as i:
                for s in range(2):
                    pe.wait_ge(wlo_ready, 2 * i + (s + 1))
                    for c in range(DC):
                        if c % 4 == 0:
                            pe.wait_ge(lo_ready, 4 * i + (2 * NK + 2 * s + c // 4 + 1))
                        for (a, w) in ((0, w_hi), (0, w_lo), (1, w_hi)):
                            vv = parts[:, 2 * s + c // 4, a, (c % 4) * P:(c % 4 + 1) * P]
                            last = mm(bank[c][:, 0:NP], vv, w[:, s, :], start=False, stop=False,
                                      skip_group_check=True)
                        if c % 4 == 3:
                            last.then_inc(parts_used, 1)
            pe.wait_ge(yT_ready, 1 + DC)
            for t, (t0, n) in enumerate(TILES):
                for i in range(2):
                    k = 2 * t + i
                    b = bank[k]
                    for c in range(4):
                        last = nc.tensor.transpose(b[:n, c * P:(c + 1) * P], y_t[:, 4 * i + c, t0:t0 + n],
                                                   ident[:, :])
                    last.then_inc(yj_full, 1)

        @block.scalar
        def _(act):
            link = chain(act, ach)
            A = nc.scalar.activation

            act.wait_ge(ln_var, 1)
            A(rstd[:, 3:6], rstd[:, 0:3], ACT.Sqrt).then_inc(ln_std, 1)
            act.wait_ge(cols_sem, 32)
            A(dt_, col("ldt"), ACT.Exp).then_inc(dt_ready, 1)
            act.wait_ge(zr_ready, 1)
            A(mag, zr, ACT.Exp).then_inc(mag_ready, 1)
            act.wait_ge(lb_arg, 1)
            A(lbv[:, 0:8], lbv[:, 0:8], ACT.Exp).then_inc(lb_exp, 1)
            act.wait_ge(sin_arg, 1)
            A(sn, r_, ACT.Sin)
            A(cs, absr, ACT.Sin).then_inc(sin_ready, 1)

            for t, (t0, n) in enumerate(TILES):
                for i in range(2):
                    computed(act, "xT", t, i)
                    readout(A(x_t[:, 4 * i:4 * i + 4, t0:t0 + n],
                              bank_of("xT", t, i)[:, 0:4 * n].rearrange("p (c n) -> p c n", n=n), ACT.Copy),
                            "xT", t, i)
            for m in range(4):
                computed(act, "u", m)
                b = bank_of("u", m)
                bias = col("bu")[:, m:m + 1]
                A(u_chan[:, m, :, 0:NB], b[:, NPROMPT:NT].rearrange("p (n j) -> p j n", j=SC),
                  ACT.Identity, bias=bias)
                readout(A(u_chan[:, m, :, NB:NCH], b[:, 0:NPROMPT].rearrange("p (n j) -> p j n", j=SC),
                          ACT.Identity, bias=bias), "u", m)
            act.wait_ge(cpow_ready, 1)
            act.wait_ge(lb_arg, 2)
            for m in range(4):
                computed(act, "f", m)
                b = bank_of("f", m)
                A(f_t[:, m, :], b[:, 0:NT], ACT.Sigmoid, bias=col("bf")[:, m:m + 1])
                readout(A(k_t[:, m, :], b[:, 0:NT], ACT.Sigmoid, bias=lbv[:, 12 + m:13 + m], scale=-1.0), "f", m)
            for b8 in range(8):
                computed(act, "w1T", b8)
                readout(A(w1_t[:, :, :, :].rearrange("p r a s -> p (r a s)")[:, b8 * 512:(b8 + 1) * 512],
                          bank_of("w1T", b8)[:, :], ACT.Copy), "w1T", b8)
            act.wait_ge(zeroed, 3)
            for b4 in range(4):
                computed(act, "toep", b4)
                b = bank_of("toep", b4)[:, :].rearrange("p (k s) -> p k s", s=P)
                for i in range(SC):
                    last = A(toep[32 * i:32 * i + 32, 4 * b4:4 * b4 + 4, 32 * i:P],
                             b[32 * i:32 * i + 32, :, 32 * i:P], ACT.Copy)
                readout(last, "toep", b4)
            for m in range(4):
                computed(act, "q", m)
                readout(A(q_t[:, m, :], bank_of("q", m)[:, 0:NT], ACT.Identity, bias=col("bq")[:, m:m + 1]), "q", m)
            xf = x_s5[:, :, :, :].rearrange("p r a n -> p (r a n)")
            act.wait_ge(cpow_ready, 1)
            act.wait_ge(w1_ready, 1)
            for b6 in range(6):
                computed(act, "X", b6)
                n = min(6, 32 - 6 * b6) * NCH
                readout(A(xf[:, 6 * b6 * NCH:6 * b6 * NCH + n], bank_of("X", b6)[:, 0:n], ACT.Copy), "X", b6)
            for t, (t0, n) in enumerate(TILES):
                evacuated(act, "gate", t)
                A(gate_sig[:n, t, :], gate[:n, t, :], ACT.Sigmoid).then_inc(gate_s, 1)
            for b3 in range(3):
                evacuated(act, "y", b3)
                n = min(6, NPAIR - 6 * b3)
                A(z4[:, 6 * b3:6 * b3 + n, :], z4[:, 6 * b3:6 * b3 + n, :], ACT.Gelu_apprx_tanh).then_inc(z_ready, 1)
            evacuated(act, "v", 2)
            computed(act, "y", 2)
            for g in range(9):
                A(v_mask[:, g, :], v_tok[:48, 2, :], ACT.Copy, scale=lane[:48, g:g + 1]).then_inc(vm_ready, 1)
            act.wait_ge(gate_done, 3)
            for t, (t0, n) in enumerate(TILES):
                computed(act, "kend", t)
                readout(A(k_end[:n, t, :, :], bank_of("kend", t)[:n, :].rearrange("p (h k) -> p h k", k=P),
                          ACT.Copy), "kend", t)
            act.wait_ge(fins_ready, 1)
            for t, (t0, n) in enumerate(TILES):
                computed(act, "o", t)
                readout(A(o_tok[:n, t, :], bank_of("o", t)[:n, :], ACT.Copy), "o", t)
            act.wait_ge(ms_ready, 1)
            A(rms[:, :], rms[:, :], ACT.Sqrt).then_inc(rms_ready, 1)
            for m in range(4):
                computed(act, "glu", m)
                b = bank_of("glu", m)
                readout(A(du[:, 4 * m:4 * m + 4, :].rearrange("p a n -> p (a n)"), b[:, 0:NT], ACT.Sigmoid,
                          bias=col("bglu")[:, m:m + 1]), "glu", m)
            for t, (t0, n) in enumerate(TILES):
                computed(act, "oT", t)
                readout(A(ohg_t[:, :, t0:t0 + n], bank_of("oT", t)[:, 0:4 * n].rearrange("p (h n) -> p h n", n=n),
                          ACT.Copy), "oT", t)
            act.wait_ge(ln_var, 2)
            A(rstd[:, 3:6], rstd[:, 0:3], ACT.Sqrt).then_inc(ln_std, 1)
            for t, (t0, n) in enumerate(TILES):
                for i in range(2):
                    computed(act, "x1T", t, i)
                    readout(A(x1_t[:, 4 * i:4 * i + 4, t0:t0 + n],
                              bank_of("x1T", t, i)[:, 0:4 * n].rearrange("p (c n) -> p c n", n=n), ACT.Copy),
                            "x1T", t, i)
            evacuated(act, "Sb", NB - 1)
            evacuated(act, "S", 2)
            for g in range(4):
                for m in range(4):
                    computed(act, "Q", 4 * g + m)
                    readout(A(q_peer[:, 4 * g + m, :], bank_of("Q", 4 * g + m)[:, 0:NT], ACT.Copy), "Q", 4 * g + m)
                for t, (t0, n) in enumerate(TILES):
                    computed(act, "sc", g, t)
                    readout(A(scores[:n, t, 4 * g:4 * g + 4, :],
                              bank_of("sc", g, t)[:n, :].rearrange("p (m k) -> p m k", k=NK), ACT.Copy), "sc", g, t)
            act.sem_inc(gelu_done, 4)
            def high_part(i, q):
                s = q // 2
                if q % 2 == 0:
                    act.wait_ge(uv_landed[s % 4], 16 * i + 16 * (s // 4 + 1))
                act.wait_ge(parts_used, 8 * i + (q + 1))
                A(parts[:, q % 4, 0, :], raw[:, s % 4, (q % 2) * 512:(q % 2 + 1) * 512], ACT.Copy
                  ).then_inc(hi_ready, 1)

            def u_blocks(i):
                for s in range(4):
                    high_part(i, 2 * s + 4)
                    high_part(i, 2 * s + 5)
                    act.wait_ge(parts_used, 8 * i + (2 * s + 6))
                    A(store[:, bass.ds(4 * i + s, 1), :].squeeze(1), bank[s][:, 0:NP],
                      ACT.Gelu_apprx_tanh).then_inc(gelu_done, 1)

            for q in range(4):
                high_part(0, q)
            with act.Fori(0, SPLIT // 4 - 4, 1) as i:
                u_blocks(i)
            act.wait_ge(tk_neg, 1)
            A(tk_sc[:, :, :, :], tk_sc[:, :, :, :], ACT.Exp).then_inc(tk_exp, 1)
            with act.Fori(SPLIT // 4 - 4, SPLIT // 4, 1) as i:
                u_blocks(i)
            act.wait_ge(idxT_full, 3)
            with act.Fori(SPLIT // 4, NK // 4, 1) as i:
                u_blocks(i)
            act.wait_ge(zero_ready, 1)

            def w_high(i, s):
                act.wait_ge(parts_used, 8 * i + (2 * NK + 2 * s + 2))
                A(w_hi[:, s % 2, :], store[:, bass.ds(4 * i + s, 1), :].squeeze(1), ACT.Copy
                  ).then_inc(whi_ready, 1)

            w_high(0, 0)
            w_high(0, 1)
            with act.Fori(0, NK // 4 - 1, 1) as i:
                for s in range(2, 6):
                    high_part(i + NK // 4, 2 * s)
                    high_part(i + NK // 4, 2 * s + 1)
                    w_high(i, s)
            for s in range(2, 4):
                high_part(2 * NK // 4 - 1, 2 * s)
                high_part(2 * NK // 4 - 1, 2 * s + 1)
                w_high(NK // 4 - 1, s)
            act.wait_ge(parts_used, 4 * NK + 4)
            act.wait_ge(yT_ready, 1)
            for c in range(0, DC, 2):
                A(y_t[:, c, META:NT], bank[c][:, 0:NP], ACT.Copy).then_inc(yT_ready, 1)
            act.wait_ge(ln_var, 3)
            A(rstd[:, 3:6], rstd[:, 0:3], ACT.Sqrt).then_inc(ln_std, 1)

        @block.vector
        def _(dve):
            link = chain(dve, dch)
            V = dve

            def layer_norm(rows, k, ready):
                for t, (t0, n) in enumerate(TILES):
                    for i in range(2):
                        last = V.bn_stats(stats[:n, 12 * t + 6 * i:12 * t + 6 * i + 6],
                                          x_tok[:n, t, 512 * i:512 * (i + 1)])
                    link(last)
                    link(V.bn_aggr(mv[:n, 2 * t:2 * t + 2], stats[:n, 12 * t:12 * t + 12]))
                    link(V.tensor_scalar(rstd[:n, t:t + 1], mv[:n, 2 * t + 1:2 * t + 2], LN_EPS, None, ALU.add))
                V.tensor_copy(rstd[:, 3:6], rstd[:, 0:3]).then_inc(ln_var, 1)
                dve.wait_ge(ln_std, k)
                link(V.reciprocal(rstd[:, 3:6], rstd[:, 3:6]))
                for t, (t0, n) in enumerate(TILES):
                    x = x_tok[:n, t, :]
                    link(V.tensor_scalar(x, x, mv[:n, 2 * t:2 * t + 1], rstd[:n, 3 + t:4 + t],
                                         ALU.subtract, ALU.mult))
                    link(V.tensor_tensor(x, x, rows[:n, 0, :], ALU.mult))
                    V.tensor_tensor(x, x, rows[:n, 1, :], ALU.add).then_inc(ready, 1)

            V.memset(rms[:, :], 1.0)
            link(V.memset(rstd[:, :], 1.0))
            dve.wait_ge(x_in, 80)
            dve.wait_ge(rows_sem, 32)
            layer_norm(rows_emb, 1, x0_ready)

            dve.wait_ge(cols_sem, 32)
            dve.wait_ge(dt_ready, 1)
            V.tensor_tensor(zr, col("are"), dt_, ALU.mult).then_inc(zr_ready, 1)
            link(V.tensor_tensor(zi, col("aim"), dt_, ALU.mult))
            link(V.tensor_scalar(kk_, zi, 0.15915494309189535, ROUND, ALU.mult, ALU.add))
            link(V.tensor_scalar(kk_, kk_, ROUND, None, ALU.subtract))
            link(V.scalar_tensor_tensor(r_, kk_, -TWO_PI_HI, zi, ALU.mult, ALU.add))
            link(V.scalar_tensor_tensor(r_, kk_, -TWO_PI_MID, r_, ALU.mult, ALU.add))
            link(V.scalar_tensor_tensor(r_, kk_, -TWO_PI_LO, r_, ALU.mult, ALU.add))
            link(V.tensor_scalar(r_, r_, -PI_IN, PI_IN, ALU.max, ALU.min))
            link(V.tensor_scalar(t1, r_, -1.0, None, ALU.mult))
            link(V.tensor_tensor(t1, t1, r_, ALU.max))
            V.tensor_scalar(absr, t1, -1.0, 1.5707963267948966, ALU.mult, ALU.add).then_inc(sin_arg, 1)
            link(V.tensor_tensor(lbv[:, 20:24], col("lb0"), col("lb1"), ALU.max))
            V.tensor_tensor(lbv[:, 0:4], col("lb0"), lbv[:, 20:24], ALU.subtract)
            V.tensor_tensor(lbv[:, 4:8], col("lb1"), lbv[:, 20:24], ALU.subtract).then_inc(lb_arg, 1)
            V.tensor_tensor(den, col("are"), col("are"), ALU.mult)
            link(V.tensor_tensor(t2, col("aim"), col("aim"), ALU.mult))
            link(V.tensor_tensor(den, den, t2, ALU.add))
            link(V.reciprocal(den, den))
            dve.wait_ge(lb_exp, 1)
            link(V.tensor_tensor(lbv[:, 20:24], lbv[:, 0:4], lbv[:, 4:8], ALU.add))
            link(V.reciprocal(lbv[:, 20:24], lbv[:, 20:24]))
            V.tensor_tensor(lbv[:, 8:12], lbv[:, 0:4], lbv[:, 20:24], ALU.mult)
            link(V.tensor_scalar(lbv[:, 12:16], col("bf"), -1.0, None, ALU.mult))
            V.tensor_scalar(lbv[:, 16:20], lbv[:, 8:12], -1.0, 1.0, ALU.mult, ALU.add).then_inc(lb_arg, 1)
            dve.wait_ge(sin_ready, 1)
            dve.wait_ge(mag_ready, 1)
            V.tensor_tensor(ar, mag, cs, ALU.mult)
            V.tensor_tensor(ai, mag, sn, ALU.mult).then_inc(abar_ready, 1)
            dve.wait_ge(abar_ready, 1)
            link(V.tensor_scalar(nr, ar, -1.0, None, ALU.add))
            tiny = (t1, t2, cr, ci)
            cmul_conj(V, link, (p2r, p2i), (nr, ai), (col("are"), col("aim")), tiny)
            V.tensor_tensor(cr, p2r, den, ALU.mult)
            link(V.tensor_tensor(ci, p2i, den, ALU.mult))
            c4 = [cm[:, k, :].rearrange("p (a c) -> p a c", c=16) for k in range(4)]
            braw = [s5raw[:, r, :, :] for r in range(2)]
            cmul(V, link, (w1c[:, 0, :, 3, :], w1c[:, 1, :, 3, :]), braw, (wide(cr, 16), wide(ci, 16)), c4)
            for j in (2, 1, 0):
                cmul(V, link, (w1c[:, 0, :, j, :], w1c[:, 1, :, j, :]),
                     (w1c[:, 0, :, j + 1, :], w1c[:, 1, :, j + 1, :]), (wide(ar, 16), wide(ai, 16)), c4)
            dve.wait_ge(zeroed, 1)
            for g in range(2):
                h = slice(64 * g, 64 * g + 64)
                last = V.tensor_copy(w1[h, :, :, :, g, :].rearrange("p r a j c -> p (r a) j c"),
                                     w1c[h, :, :, :, :].rearrange("p r a j c -> p (r a) j c"))
            last.then_inc(w1_ready, 1)
            tiny = (t1, t2, nr, den)
            cmul(V, link, (p2r, p2i), a_bar, a_bar, tiny)
            cmul(V, link, (a4r, a4i), (p2r, p2i), (p2r, p2i), tiny)
            link(V.tensor_tensor(m4, mag, mag, ALU.mult))
            link(V.tensor_tensor(m4, m4, m4, ALU.mult))
            link(V.tensor_copy(decay[:, :, :], wide(m4, NCP)))
            link(V.memset(decay[:, :, 0:1], 0.0))

            dve.wait_ge(lb_arg, 2)
            for m in range(HEADS):
                evacuated(dve, "f", m)
                oml = lbv[:, 16 + m:17 + m]
                V.tensor_scalar(f_t[:, m, :], f_t[:, m, :], oml, lbv[:, 8 + m:9 + m], ALU.mult, ALU.add)
                V.tensor_scalar(k_t[:, m, :], k_t[:, m, :], oml, None, ALU.mult).then_inc(f_pre, 1)
            dve.wait_ge(f_pre, 4)
            V.tensor_copy(pre[:, :, :], f_t[:, :, :])
            link(V.memset(suf[:, :, :], 1.0))

            for b6 in range(6):
                evacuated(dve, "X", b6)
            dve.wait_ge(rot_ready, 1)
            computed(dve, "toep", 3)
            computed(dve, "X", 5)
            X = [x_s5[:, r, :, :] for r in range(2)]
            G = [g_s5[:, r, :, :] for r in range(2)]
            H = [h_in[:, r, :, :] for r in range(2)]
            R = [rot[:, r, :, :] for r in range(2)]
            T = [cm_scan[:, r, :, :] for r in range(2)]
            for r, (op, other) in enumerate(((ALU.add, 1), (ALU.subtract, 0))):
                V.tensor_tensor(T[0], X[r][:, :, NB:NCH], R[0], ALU.mult)
                link(V.tensor_tensor(T[1], X[other][:, :, NB:NCH], R[1], ALU.mult))
                link(V.tensor_tensor(G[r], T[0], T[1], op))
            df = decay[:, :, :].rearrange("p a n -> p (a n)")
            for r in range(2):
                gf = G[r].rearrange("p a n -> p (a n)")
                last = V.tensor_tensor_scan(gf, df, gf, 0.0, ALU.mult, ALU.add)
            link(last)
            h0 = col("h0").rearrange("p (r a b) -> p r a b", r=2, b=NB)
            f8 = [cm[:, k, 0:128].rearrange("p (a b) -> p a b", b=NB) for k in range(4)]
            cmul(V, link, (fins[:, 0, :, 0:NB], fins[:, 1, :, 0:NB]), (h0[:, 0], h0[:, 1]),
                 (wide(a4r, NB), wide(a4i, NB)), f8)
            for r in range(2):
                last = V.tensor_tensor(fins[:, r, :, 0:NB], fins[:, r, :, 0:NB], X[r][:, :, 0:NB], ALU.add)
            link(last)
            for r, (op, other) in enumerate(((ALU.subtract, 1), (ALU.add, 0))):
                o = 1 - other if r == 0 else 1
                V.tensor_tensor(T[0], G[r], R[0], ALU.mult)
                link(V.tensor_tensor(T[1], G[other], R[1], ALU.mult))
                V.tensor_tensor(H[r][:, :, NB + 1:NCH], T[0][:, :, 0:NCP - 1], T[1][:, :, 0:NCP - 1], op)
                V.tensor_tensor(fins[:, r, :, NB:NB + 1], T[0][:, :, NCP - 1:NCP], T[1][:, :, NCP - 1:NCP], op)
                V.tensor_copy(H[r][:, :, 0:NB], h0[:, r])
                link(V.memset(H[r][:, :, NB:NB + 1], 0.0))
            V.sem_inc(hin_ready, 1)
            V.sem_inc(fins_ready, 1)
            dve.wait_ge(u4_moved, 16 * 16)
            link(V.tensor_tensor(du[:, :, :], u4[:, :, :], wide(col("d"), NCH), ALU.mult))

            dve.wait_ge(rowsv_sem, 32)
            for t, (t0, n) in enumerate(TILES):
                computed(dve, "v", t)
                readout(V.tensor_tensor(v_tok[:n, t, :], bank_of("v", t)[:n, :], rows_v[:n, 0, :], ALU.add), "v", t)
            for t, (t0, n) in enumerate(TILES):
                computed(dve, "gate", t)
                readout(V.tensor_tensor(gate[:n, t, :], bank_of("gate", t)[:n, :], rows_v[:n, 1, :], ALU.add),
                        "gate", t)

            dve.wait_ge(zeroed, 4)
            dve.wait_ge(masks_sem, 16)

            def pick(h):
                for t in level_tiles(h):
                    n = TILES[t][1]
                    computed(dve, "att", h, t)
                    b = bank_of("att", h, t)[:, :].rearrange("p (h s) -> p h s", s=P)
                    if h <= 16:
                        last = V.copy_predicated(att[:n, t, :, 0:n], mask(h, t), b[:n, :, 0:n])
                    elif h == 32:
                        V.tensor_copy(att[0:32, t, :, 32:64], b[0:32, :, 32:64])
                        last = V.tensor_copy(att[64:96, t, :, 96:128], b[64:96, :, 96:128])
                    else:
                        last = V.tensor_copy(att[0:64, t, :, 64:128], b[0:64, :, 64:128])
                    readout(last, "att", h, t)

            def gate_finish():
                for t, (t0, n) in enumerate(TILES):
                    dve.wait_ge(gate_s, t + 1)
                    link(V.tensor_tensor(gate[:n, t, :], gate[:n, t, :], gate_sig[:n, t, :], ALU.mult))
                    V.tensor_tensor(gate[:n, t, :], gate[:n, t, :], rows_v[:n, 2, :], ALU.mult).then_inc(gate_done, 1)

            pick(0)
            for b3 in range(3):
                computed(dve, "y", b3)
                n = min(6, NPAIR - 6 * b3)
                a = slice(6 * b3, 6 * b3 + n)
                readout(V.tensor_tensor(z4[:, a, :], bank_of("y", b3)[:, 0:n * NCH].rearrange("p (a n) -> p a n", n=NCH),
                                        du[:, a, :], ALU.add), "y", b3)
            for m in range(HEADS):
                evacuated(dve, "q", m)
            for lv, h in enumerate(LEVELS[1:]):
                cols_n = NT if h <= 8 else 2 * P
                V.tensor_tensor(q_dec[:, :, 0:cols_n], q_t[:, :, 0:cols_n], pre[:, :, 0:cols_n], ALU.mult)
                V.tensor_tensor(k_dec[:, :, 0:cols_n], k_t[:, :, 0:cols_n], suf[:, :, 0:cols_n],
                                ALU.mult).then_inc(lvl_ready, 1)
                lim = NT if h <= 2 else NPROMPT if h <= 8 else 2 * P
                pv = pre[:, :, 0:lim].rearrange("p h (b s k) -> p h b s k", s=2, k=h)
                sv = suf[:, :, 0:lim].rearrange("p h (b s k) -> p h b s k", s=2, k=h)
                shape = [P, lim // (2 * h), h]
                dve.wait_ge(lvl_ready, lv + 1)
                for hd in range(HEADS):
                    last = V.tensor_tensor(sv[:, hd, :, 0, :], sv[:, hd, :, 0, :],
                                           pv[:, hd, :, 1, h - 1:h].broadcast_to(shape), ALU.mult)
                link(last)
                for hd in range(HEADS):
                    last = V.tensor_tensor(pv[:, hd, :, 1, :], pv[:, hd, :, 1, :],
                                           pv[:, hd, :, 0, h - 1:h].broadcast_to(shape), ALU.mult)
                link(last)
                pick(h)
            V.tensor_tensor(q_dec[:, :, :], q_t[:, :, :], pre[:, :, :], ALU.mult)
            V.tensor_tensor(k_dec[:, :, :], k_t[:, :, :], suf[:, :, :], ALU.mult).then_inc(pre_done, 1)
            gate_finish()

            computed(dve, "S", 0)
            readout(V.tensor_copy(s_prompt[:, :, :].rearrange("p h v -> p (h v)"), bank_of("S", 0)[:, :]), "S", 0)
            for t in (1, 2):
                computed(dve, "S", t)
                last_col = (2 * P if t == 1 else NPROMPT) - 1
                evacuated(dve, "S", t - 1)
                for hd in range(HEADS):
                    last = V.scalar_tensor_tensor(s_prompt[:, hd, :], s_prompt[:, hd, :],
                                                  pre[:, hd, last_col:last_col + 1],
                                                  bank_of("S", t)[:, hd * P:(hd + 1) * P], ALU.mult, ALU.add)
                readout(last, "S", t)
            for t, (t0, n) in enumerate(TILES):
                evacuated(dve, "o", t)
                link(V.tensor_tensor(o_sq[:n, :], o_tok[:n, t, :], o_tok[:n, t, :], ALU.mult))
                link(V.reduce_sum(rms[:n, 4 * t:4 * t + 4], o_sq[:n, :].rearrange("p (h v) -> p h v", v=P), AX))
            V.tensor_scalar(rms[:, :], rms[:, :], 1.0 / P, RMS_EPS, ALU.mult, ALU.add).then_inc(ms_ready, 1)
            dve.wait_ge(s0_scaled, 1)
            for g in range(NB):
                computed(dve, "Sb", g)
                sg = s_samp[:, g, :, :].rearrange("p h v -> p (h v)")
                readout(V.tensor_tensor(sg, sg, bank_of("Sb", g)[:, :], ALU.add), "Sb", g)
            dve.wait_ge(rms_ready, 1)
            link(V.reciprocal(rms[:, :], rms[:, :]))
            for t, (t0, n) in enumerate(TILES):
                ot = o_tok[:n, t, :].rearrange("p (h v) -> p h v", v=P)
                link(V.tensor_tensor(ot, ot, rms[:n, 4 * t:4 * t + 4].unsqueeze(2).broadcast_to([n, HEADS, P]),
                                     ALU.mult))
                V.tensor_tensor(o_tok[:n, t, :], o_tok[:n, t, :], gate[:n, t, :], ALU.mult).then_inc(og_ready, 1)

            for m in range(4):
                evacuated(dve, "glu", m)
                sg = du[:, 4 * m:4 * m + 4, :]
                V.tensor_tensor(ossm_t[:, m, 0:NPROMPT].rearrange("p (n j) -> p j n", j=SC),
                                z_t[:, m, :, NB:NCH], sg[:, :, NB:NCH], ALU.mult)
                V.tensor_tensor(ossm_t[:, m, NPROMPT:NT].rearrange("p (n j) -> p j n", j=SC),
                                z_t[:, m, :, 0:NB], sg[:, :, 0:NB], ALU.mult).then_inc(glu_s, 1)

            for i in range(2):
                for t, (t0, n) in enumerate(TILES):
                    computed(dve, "mix", t, i)
                    xx = x_tok[:n, t, 512 * i:512 * (i + 1)]
                    readout(V.scalar_tensor_tensor(xx, xx, ALPHA, bank_of("mix", t, i)[:n, :], ALU.mult, ALU.add),
                            "mix", t, i)
            for t in range(3):
                evacuated(dve, "mix", t, 1)
            dve.wait_ge(rows1_sem, 32)
            layer_norm(rows_ln1, 2, x1_ready)

            link(V.memset(tk_sc[:, :, :, :], 0.0))

            def top16(n, srcs):
                for half in range(2):
                    k = slice(8 * half, 8 * half + 8)
                    for s, v, ix in srcs:
                        last = V.max(v[:, k], s)
                    link(last)
                    for s, v, ix in srcs:
                        last = V.max_index(ix[:, k], v[:, k], s)
                    if half == 0:
                        link(last)
                        for s, v, ix in srcs:
                            last = V.match_replace(s, v[:, k], s, LOWEST)
                    link(last)

            for g in range(4):
                for t, (t0, n) in enumerate(TILES):
                    evacuated(dve, "sc", g, t)
                    top16(n, [(scores[:n, t, 4 * g + m, :], tk_val[:n, m, :], tk_idx[:n, m, :]) for m in range(4)])
                    v = tk_val[:n, :, :].rearrange("p (h c) k -> p h c k", c=2)
                    V.tensor_copy(tk_idxf[:n, :, :], tk_idx[:n, :, :])
                    link(V.tensor_tensor(tk_cand[:n, :, :, :],
                                         v[:, :, 0, :].unsqueeze(3).broadcast_to([n, 2, TOPK, TOPK]),
                                         v[:, :, 1, :].unsqueeze(2).broadcast_to([n, 2, TOPK, TOPK]), ALU.add))
                    top16(n, [(tk_cand[:n, h, :, :].rearrange("p a b -> p (a b)"), tk_sc[:n, t, 2 * g + h, :],
                               tk_ci[:n, h, :]) for h in range(2)])
                    V.tensor_scalar(tk_ab[:n, 0, :, :], tk_ci[:n, :, :], 4, None, ALU.logical_shift_right)
                    link(V.tensor_scalar(tk_ab[:n, 1, :, :], tk_ci[:n, :, :], 15, None, ALU.bitwise_and))
                    link(V.tensor_copy(tk_abf[:n, :, :, :], tk_ab[:n, :, :, :]))
                    keys_of = tk_idxf[:n, :, :].rearrange("p (h c) k -> p h c k", c=2)
                    for c in range(2):
                        e = tk_eq[:n, c, :, :, :].rearrange("p h k a -> p (h k) a")
                        last = V.tensor_tensor(
                            e, tk_abf[:n, c, :, :].rearrange("p h k -> p (h k)").unsqueeze(2).broadcast_to([n, 32, TOPK]),
                            iota[:n, 0:TOPK].unsqueeze(1).broadcast_to([n, 32, TOPK]), ALU.is_equal)
                    link(last)
                    for c in range(2):
                        e = tk_eq[:n, c, :, :, :]
                        last = V.tensor_tensor(e, e, keys_of[:, :, c, :].unsqueeze(2).broadcast_to([n, 2, TOPK, TOPK]),
                                               ALU.mult)
                    link(last)
                    for c in range(2):
                        link(V.reduce_sum(idx_f[:n, t, c, 32 * g:32 * g + 32],
                                          tk_eq[:n, c, :, :, :].rearrange("p h k a -> p (h k) a"), AX))
            scv = tk_sc[:, :, :, :].rearrange("p t h k -> p (t h) k")
            link(V.tensor_copy(tk_sum[:, :], scv[:, :, 0:1].squeeze(2)))
            V.tensor_tensor(scv, scv, tk_sum[:, :].unsqueeze(2).broadcast_to([P, 24, TOPK]),
                            ALU.subtract).then_inc(tk_neg, 1)
            dve.wait_ge(tk_exp, 1)
            link(V.reduce_sum(tk_sum[:, :], scv, AX))
            link(V.reciprocal(tk_sum[:, :], tk_sum[:, :]))
            for t in range(3):
                V.tensor_tensor(idx_f[:, t, 2, :].rearrange("p (h k) -> p h k", k=TOPK), tk_sc[:, t, :, :],
                                tk_sum[:, 8 * t:8 * t + 8].unsqueeze(2).broadcast_to([P, PH, TOPK]),
                                ALU.mult).then_inc(idx_ready, 1)

            dve.wait_ge(idxT_full, 3)
            dve.wait_ge(gelu_done, NK + 4)
            for t, (t0, n) in enumerate(TILES):
                b = bank[5 + t]
                V.tensor_copy(idx_t[:, 0, t0:t0 + n], b[:, 0:n])
                V.tensor_copy(idx_t[:, 1, t0:t0 + n], b[:, n:2 * n])
                last = V.tensor_copy(g_all[:, t0:t0 + n], b[:, 2 * n:3 * n])
            link(last)
            link(V.tensor_copy(g_hi[:, :], g_all[:, :]))
            link(V.tensor_tensor(g_lo[:, :], g_all[:, :], g_hi[:, :].bitcast(F32), ALU.subtract))

            V.sem_inc(g_used, 2)
            g_hi32 = g_hi[:, :].bitcast(F32)
            with V.Fori(0, NP // 8, 1) as i:
                for u in range(8):
                    dve.wait_ge(hot_used, 8 * i + (u + 1))
                    tc = bass.ds(8 * i + (u + META), 1)
                    V.tensor_scalar(hot1[:, u, :], iota[:, :], idx_t[:, 0, tc], None, ALU.is_equal).then_inc(hot_ready, 1)
                    V.tensor_scalar(hot_hi[:, u, :], iota[:, :], idx_t[:, 1, tc], g_hi32[:, tc],
                                    ALU.is_equal, ALU.mult).then_inc(hot_ready, 1)
                    V.tensor_scalar(hot_lo[:, u, :], iota[:, :], idx_t[:, 1, tc], g_lo[:, tc],
                                    ALU.is_equal, ALU.mult).then_inc(hot_ready, 1)
                for k in range(2):
                    dve.wait_ge(hot_used, 8 * i + (8 + 4 * (k + 1)))
                    st = store[:, :, bass.ds(8 * i + 4 * k, 4)]
                    V.tensor_tensor(st, st, bank[3 + k][:, :].rearrange("p (t j) -> p j t", j=NK),
                                    ALU.mult).then_inc(g_used, 1)
            dve.wait_ge(g_used, 2 + NP // 4)
            V.memset(zero[:, :], 0.0).then_inc(zero_ready, 1)

            with V.Fori(0, NK // 2, 1) as i:
                for s in range(2):
                    dve.wait_ge(whi_ready, 2 * i + (s + 1))
                    V.tensor_tensor(w_lo[:, s, :], store[:, bass.ds(2 * i + s, 1), :].squeeze(1),
                                    w_hi[:, s, :].bitcast(F32), ALU.subtract).then_inc(wlo_ready, 1)

            dve.wait_ge(parts_used, 4 * NK + 4)
            V.memset(y_t[:, :, 0:META], 0.0).then_inc(yT_ready, 1)
            for c in range(1, DC, 2):
                V.tensor_copy(y_t[:, c, META:NT], bank[c][:, 0:NP]).then_inc(yT_ready, 1)
            for t, (t0, n) in enumerate(TILES):
                for i in range(2):
                    k = 2 * t + i
                    dve.wait_ge(yj_full, k + 1)
                    xx = x_tok[:n, t, 512 * i:512 * (i + 1)]
                    V.scalar_tensor_tensor(xx, xx, ALPHA, bank[k][:n, :], ALU.mult, ALU.add).then_inc(yj_read, 1)
            dve.wait_ge(yj_read, 6)
            dve.wait_ge(rows2_sem, 32)
            layer_norm(rows_ln2, 3, y_out_ready)

        @block.gpsimd
        def _(pool):
            link = chain(pool, pch)
            G = pool
            G.memset(w1[:, :, :, :, :, :].rearrange("p r a j g c -> p (r a j g c)"), 0.0).then_inc(zeroed, 1)
            G.memset(c_pow[:, :, :, :, :, :].rearrange("p r a t g c -> p (r a t g c)"), 0.0).then_inc(zeroed, 1)
            G.memset(toep[:, :, :].rearrange("p a s -> p (a s)"), 0.0).then_inc(zeroed, 1)
            pool.wait_ge(abar_ready, 1)
            pool.wait_ge(cols_sem, 32)
            p4 = [pool_tmp[:, k, :].rearrange("p (a c) -> p a c", c=16) for k in range(4)]
            G.tensor_copy(c_cmp[:, 0, :, 0, :], s5raw[:, 2, :, :])
            link(G.tensor_scalar(c_cmp[:, 1, :, 0, :], s5raw[:, 3, :, :], -1.0, None, ALU.mult))
            for t in range(4):
                cmul_conj(G, link, (c_cmp[:, 0, :, t + 1, :], c_cmp[:, 1, :, t + 1, :]),
                     (c_cmp[:, 0, :, t, :], c_cmp[:, 1, :, t, :]), (wide(ar, 16), wide(ai, 16)), p4)
            pool.wait_ge(zeroed, 2)
            for g in range(2):
                h = slice(64 * g, 64 * g + 64)
                for r in range(2):
                    last = G.tensor_copy(c_pow[h, r, :, :, g, :], c_cmp[h, r, :, :, :])
                if g == 0:
                    link(last)
            last.then_inc(cpow_ready, 1)
            pool.wait_ge(cpow_ready, 1)
            rp = [pool_tmp[:, 0, 224:240], pool_tmp[:, 1, 224:240]]
            rq = [pool_tmp[:, 2, 224:240], pool_tmp[:, 3, 224:240]]
            tiny = [pool_tmp[:, k, 240:256] for k in range(4)]
            cmul(G, link, rq, (cs, sn), (cs, sn), tiny)
            cmul(G, link, rp, rq, rq, tiny)
            G.memset(rot[:, 0, :, 0:1], 1.0)
            link(G.memset(rot[:, 1, :, 0:1], 0.0))
            size = 1
            while size < NCP:
                done = 0
                count = min(size, NCP - size)
                while done < count:
                    n = min(14, count - done)
                    src = slice(done, done + n)
                    dst = slice(size + done, size + done + n)
                    tm = [pool_tmp[:, k, 0:16 * n].rearrange("p (a n) -> p a n", n=n) for k in range(4)]
                    cmul(G, link, (rot[:, 0, :, dst], rot[:, 1, :, dst]), (rot[:, 0, :, src], rot[:, 1, :, src]),
                         (wide(rp[0], n), wide(rp[1], n)), tm)
                    done += n
                cmul(G, link, rq, rp, rp, tiny)
                rp, rq = rq, rp
                size *= 2
            G.sem_inc(rot_ready, 1)
            pool.wait_ge(w1_ready, 1)
            pool.wait_ge(hin_ready, 1)
            G.memset(att[:, :, :, :].rearrange("p t h s -> p (t h s)"), 0.0).then_inc(zeroed, 1)
            link(G.memset(q_mask[:, :, :, :].rearrange("p g h s -> p (g h s)"), 0.0))
            pool.wait_ge(pre_done, 1)
            G.tensor_copy(q_mask[:, 0, :, 0:T2P], q_dec[:, :, 2 * P:NPROMPT])
            for b in range(NB):
                c = T2P + NS * b
                last = G.tensor_copy(q_mask[:, 1 + b, :, c:c + NS], q_dec[:, :, 2 * P + c:2 * P + c + NS])
            last.then_inc(qm_ready, 1)
            computed(pool, "o", 2)
            tot = pre[:, :, NPROMPT:NT].rearrange("p h (b j) -> p b h j", j=NS)[:, :, :, NS - 1:NS]
            for b in range(NB):
                last = G.tensor_tensor(s_samp[:, b, :, :], s_samp[:, b, :, :],
                                       tot[:, b, :, :].broadcast_to([P, HEADS, P]), ALU.mult)
            last.then_inc(s0_scaled, 1)
            for t in range(3):
                for i in range(2):
                    evacuated(pool, "x1T", t, i)
            G.tensor_copy(xw[:, 0, :, :], x1_t[:, :, META:NT]).then_inc(xw_ready, 1)
            pool.wait_ge(xw_ready, 1)
            G.tensor_tensor(xw[:, 1, :, :], x1_t[:, :, META:NT], xw[:, 0, :, :].bitcast(F32),
                            ALU.subtract).then_inc(xw_ready, 1)
            with pool.Fori(0, 2 * NK // 4, 1) as i:
                for q in range(8):
                    pool.wait_ge(hi_ready, 8 * i + (q + 1))
                    G.tensor_tensor(parts[:, q % 4, 1, :], raw[:, q // 2, (q % 2) * 512:(q % 2 + 1) * 512],
                                    parts[:, q % 4, 0, :].bitcast(F32), ALU.subtract).then_inc(lo_ready, 1)


def kernel(x_prompt, x_sample, state_hgrn, state_ssm_re, state_ssm_im, meta_tokens, ln_emb_g, ln_emb_b,
           lb_logits, w_in, b_in, hg_norm_g, ssm_a_re, ssm_a_im, ssm_log_dt, ssm_b_re, ssm_b_im,
           ssm_c_re, ssm_c_im, ssm_d, w_glu, b_glu, w_out, ln1_g, ln1_b, peer_w_q, peer_keys,
           peer_u, peer_v, ln2_g, ln2_b):
    import numpy as np
    import concourse.bacc as bacc
    from concourse.bass_utils import run_bass_kernel_spmd

    def arr(a):
        return np.asarray(a)

    def by_chunk(v):
        return arr(v).reshape(-1, P).T

    def by_state(a):
        a = arr(a)
        a = a.reshape((NPAIR, 2, 64) + a.shape[2:])
        return np.moveaxis(a, 0, 2).reshape((P, NPAIR) + a.shape[3:])

    b_in0 = arr(b_in)[0]
    log_dt = np.repeat(arr(ssm_log_dt)[0][:, None], 64, axis=1)
    d_rows = np.tile(arr(ssm_d)[0].reshape(NPAIR, 32).T, (SC, 1))
    h0 = np.stack([by_state(np.moveaxis(arr(s)[0], 0, 2)) for s in (state_ssm_re, state_ssm_im)], axis=1)
    cols = np.concatenate([by_chunk(b_in0[0:512]), by_chunk(b_in0[512:1024]), by_chunk(b_in0[2048:2560]),
                           by_chunk(arr(b_glu)[0]), by_chunk(arr(lb_logits)[0]), by_chunk(arr(lb_logits)[1]),
                           by_state(arr(ssm_a_re)[0]), by_state(arr(ssm_a_im)[0]), by_state(log_dt), d_rows,
                           h0.reshape(P, -1)], axis=1)
    s5bc = np.stack([by_state(arr(ssm_b_re)[0]), by_state(arr(ssm_b_im)[0]),
                     by_state(np.swapaxes(arr(ssm_c_re)[0], 1, 2)), by_state(np.swapaxes(arr(ssm_c_im)[0], 1, 2))],
                    axis=1).reshape(P, -1)
    hg_row = np.concatenate([arr(hg_norm_g)[0], np.zeros(512, np.float32)])
    rows = np.stack([arr(ln_emb_g), arr(ln_emb_b), b_in0[1024:2048], arr(ln1_g)[0], arr(ln1_b)[0],
                     arr(ln2_g)[0], arr(ln2_b)[0], hg_row])
    s, t = np.meshgrid(np.arange(P), np.arange(P), indexing="ij")
    full = [s == t] + [(s // (2 * h) == t // (2 * h)) & (s % (2 * h) < h) & (t % (2 * h) >= h)
                       for h in (1, 2, 4, 8, 16)]
    last = [m & ((h < 4) | ((s < T2P) & (t < T2P))) for m, h in zip(full, (0, 1, 2, 4, 8))]
    masks = np.concatenate(full + [m[:, 0:48] for m in last], axis=1).astype(np.uint8)
    masks = np.ascontiguousarray(masks).view(np.uint32)
    group = np.where(np.arange(P) < T2P, 0, 1 + (np.arange(P) - T2P) // NS)
    consts = np.concatenate([np.eye(P), np.tile(np.arange(P), (P, 1)), group[:, None] == np.arange(9)[None, :]],
                            axis=1).astype(np.float32)
    arrays = {
        "x_prompt": arr(x_prompt)[0], "x_sample": arr(x_sample).reshape(NSAMP, D), "meta": arr(meta_tokens),
        "state": arr(state_hgrn)[0], "cols": cols, "s5bc": s5bc, "rows": rows, "masks": masks, "consts": consts,
        "w_in": arr(w_in)[0], "w_glu": arr(w_glu)[0], "w_out": arr(w_out)[0], "w_q": arr(peer_w_q)[0],
        "keys": arr(peer_keys)[0].reshape(2 * PH, NK, P).transpose(2, 0, 1),
        "uv": np.concatenate([arr(peer_u)[0].reshape(NK, NK, DC, P).transpose(1, 3, 2, 0).reshape(NK, P, D),
                              arr(peer_v)[0].reshape(NK, NK, D).transpose(1, 0, 2)]),
    }
    arrays = {f"in_{k}": np.ascontiguousarray(a) for k, a in arrays.items()}
    outs = {"y_prompt": [SEQ, D], "y_sample": [NSAMP, D], "hg_prompt": [HEADS, P, P],
            "hg_sample": [NB, HEADS, P, P], "ssm": [P, 2 * NPAIR * 9]}
    nc = bacc.Bacc("TRN2", target_bir_lowering=False, num_devices=1)
    args = [nc.dram_tensor(k, a.shape, mybir.dt.from_np(a.dtype), kind="ExternalInput").ap()
            for k, a in arrays.items()]
    args += [nc.dram_tensor(f"out_{k}", sh, F32, kind="ExternalOutput").ap() for k, sh in outs.items()]
    trunk(nc, *args)
    r = run_bass_kernel_spmd(nc, [arrays], core_ids=[0]).results[0]
    ssm = np.asarray(r["out_ssm"]).reshape(2, 64, 2, NPAIR, 9).transpose(2, 4, 3, 0, 1).reshape(2, 9, 32, 64)
    return (np.asarray(r["out_y_prompt"]).reshape(1, SEQ, D), np.asarray(r["out_y_sample"]).reshape(NB, NS, D),
            np.asarray(r["out_hg_prompt"]).reshape(1, 1, HEADS, P, P), ssm[0, 8:9][None], ssm[1, 8:9][None],
            np.asarray(r["out_hg_sample"]).reshape(1, NB, HEADS, P, P), ssm[0, 0:8][None], ssm[1, 0:8][None])
```

```python
from contextlib import ExitStack

import concourse.bass as bass
from concourse import mybir
from concourse.alu_op_type import AluOpType as ALU

ACT = mybir.ActivationFunctionType
F32 = mybir.dt.float32
F32R = mybir.dt.float32r
U8 = mybir.dt.uint8
U32 = mybir.dt.uint32
AX = mybir.AxisListType.X

P = 128
D = 1024
DC = D // P
META, SEQ, NB, NS = 16, 256, 8, 4
NPROMPT = META + SEQ
NSAMP = NB * NS
NT = NPROMPT + NSAMP
TILES = [(0, 128), (128, 128), (256, 48)]
T2P = 16
HEADS = 4
DHG = 512
NPAIR = 16
SC = 4
NCH = NT // SC
NCP = NPROMPT // SC
PH = 8
NK = 128
TOPK = 16
NP = NT - META
PTILES = [(0, 128), (128, 128), (256, 32)]
QB = 2 * PH
U_ROUND = QB // 4
V_ROUND = U_ROUND + NK // 4
ROUNDS = V_ROUND + NK // 4
V_HALF = 8 * V_ROUND
BY_ACT = 3
BY_VEC = 8 - BY_ACT
ALPHA = 2.0 ** 0.25
LN_EPS = 1e-5
RMS_EPS = 1e-6
LOWEST = -3.4028234663852886e38
PI_IN = 3.1415925
TWO_PI_HI = 6.28125
TWO_PI_MID = 0.0019350051879882812
TWO_PI_LO = 3.019916050561733e-07
ROUND = 12582912.0

COLS = {}
for _name, _n in (("bq", 4), ("bf", 4), ("bu", 4), ("bglu", 4), ("lb0", 4), ("lb1", 4), ("are", 16),
                  ("aim", 16), ("ldt", 16), ("d", 16), ("h0", 2 * NPAIR * NB)):
    COLS[_name] = (sum(n for _, n in COLS.values()), _n)
NCOLS = sum(n for _, n in COLS.values())


def trunk(nc, x_prompt, x_sample, meta, state, cols_in, s5bc, rows_in, masks_in, consts_in,
          w_in, w_glu, w_out, keys_t, blocks,
          y_prompt, y_sample, hg_prompt, hg_sample, ssm_out):
    ctx = ExitStack()
    with ctx:
        ARENA = 16512

        def at(name, first, shape, dt=F32):
            return nc.alloc_sbuf_tensor_at(name, shape, dt, offset=ARENA + 4 * first)

        def sem(name):
            return ctx.enter_context(nc.semaphore(name))

        bank = [ctx.enter_context(nc.psum_tensor(f"bank{i}", [P, 512], F32)) for i in range(8)]

        w_ring = at("w_ring", 0, [P, 2, DC, 512])
        x_t = at("x_t", 8192, [P, DC, NT])
        z_t = at("z_t", 8192, [P, 4, SC, NCH])
        c_pow = at("c_pow", 10656, [P, 2, NPAIR, 5, 2, 16])
        v_mask = at("v_mask", 10656, [48, 9, DHG])
        q_peer = at("q_peer", 10656, [P, 2 * PH, NP])
        rows_v = at("rows_v", 15776, [P, 3, DHG])
        wglu = at("wglu", 15776, [P, 4, DHG])
        rows_emb = at("rows_emb", 17824, [P, 2, D])
        pool_tmp = at("pool_tmp", 19872, [P, 4, 256])
        v_tok = at("v_tok", 17824, [P, 3, DHG])
        gate = at("gate", 19360, [P, 3, DHG])
        keysT = at("keysT", 17824, [P, 2 * PH, NK])
        toep = at("toep", 20896, [P, NPAIR, P])
        rows_ln1 = at("rows_ln1", 20896, [P, 2, D])
        u_chan = at("u_chan", 22944, [P, 4, SC, NCH])
        z4 = at("z4", 22944, [P, NPAIR, NCH])
        ohg_t = at("ohg_t", 22944, [P, HEADS, NT])
        w1 = at("w1", 24160, [P, 2, NPAIR, SC, 2, 16])
        q_dec = at("q_dec", 24160, [P, HEADS, NT])
        k_dec = at("k_dec", 25376, [P, HEADS, NT])
        k_end = at("k_end", 26592, [P, 3, HEADS, P])
        w1c = at("w1c", 28256, [P, 2, NPAIR, SC, 16])
        pre = at("pre", 28256, [P, HEADS, NT])
        suf = at("suf", 29472, [P, HEADS, NT])
        scores = at("scores", 24160, [P, 3, 2 * PH, NK])
        s5raw = at("s5raw", 30688, [P, 4, NPAIR, 16])
        x_s5 = at("x_s5", 30688, [P, 2, NPAIR, NCH])
        h_in = at("h_in", 30688, [P, 2, NPAIR, NCH])
        o_tok = at("o_tok", 30688, [P, 3, DHG])
        o_sq = at("o_sq", 32224, [P, DHG])
        c_cmp = at("c_cmp", 33120, [P, 2, NPAIR, 5, 16])
        q_t = at("q_t", 33120, [P, HEADS, NT])
        k_t = at("k_t", 34336, [P, HEADS, NT])
        f_t = at("f_t", 35552, [P, HEADS, NT])
        x_tok = at("x_tok", 36864, [P, 3, D])
        ident = at("ident", 39936, [P, P])
        iota = at("iota", 40064, [P, P])
        mask_words = at("mask_words", 40192, [P, 252], U32)
        lane = at("lane", 40448, [P, 9])
        u4 = at("u4", 40600, [P, NPAIR, NCH])
        att = at("att", 41816, [P, 3, HEADS, P])
        du = at("du", 43352, [P, NPAIR, NCH])
        cols = at("cols", 44568, [P, NCOLS])
        fins = at("fins", 44912, [P, 2, NPAIR, 9])
        rot = at("rot", 45208, [P, 2, NPAIR, NCP])
        decay = at("decay", 47384, [P, NPAIR, NCP])
        ossm_t = at("ossm_t", 45208, [P, 4, NT])
        q_mask = at("q_mask", 46424, [P, 9, HEADS, 48])
        s_prompt = at("s_prompt", 48152, [P, HEADS, P])
        w1_t = at("w1_t", 48664, [P, 2, NPAIR, P])
        g_s5 = at("g_s5", 48664, [P, 2, NPAIR, NCP])
        s_samp = at("s_samp", 48664, [P, NB, HEADS, P])
        small = at("small", 52760, [P, 440])
        cm = at("cm", 41816, [P, 4, 256])
        cm_scan = at("cm_scan", 24160, [P, 2, NPAIR, NCP])
        gate_sig = at("gate_sig", 26592, [P, 3, DHG])

        store = at("store", 0, [P, NK, NP])
        xw = at("xw", 40192, [P, 2, DC, NP], F32R)
        raw = at("raw", 44800, [P, 4, D])
        parts = at("parts", 48896, [P, 4, 2, D // 2], F32R)
        idx_f = at("idx_f", 30688, [P, 3, 3, P])
        SPLIT = 80
        assert SPLIT * NP <= 24160
        tk_sc = at("tk_sc", 31840, [P, 3, PH, TOPK])
        tk_sum = at("tk_sum", 32224, [P, 3 * PH])
        tk_val = at("tk_val", 32256, [P, 4, TOPK])
        tk_idx = at("tk_idx", 32320, [P, 4, TOPK], U32)
        tk_idxf = at("tk_idxf", 32384, [P, 4, TOPK])
        tk_ci = at("tk_ci", 32448, [P, 2, TOPK], U32)
        tk_ab = at("tk_ab", 32480, [P, 2, 2, TOPK], U32)
        tk_abf = at("tk_abf", 32544, [P, 2, 2, TOPK])
        tk_cand = at("tk_cand", 32608, [P, 2, TOPK, TOPK])
        tk_eq = at("tk_eq", 33120, [P, 2, 2, TOPK, TOPK])
        idx_t = at("idx_t", 40192, [P, 3, NP])
        hot1 = at("hot1", 41056, [P, 16, P])
        hot2 = at("hot2", 43104, [P, 2, BY_VEC, P])
        apart = at("apart", 43104 + 2 * BY_VEC * P, [P, BY_ACT, P])
        hot_g = at("hot_g", 44800, [P, 16, P])
        factor = at("factor", 46848, [P, 2, 4 * P])
        assert 43104 + 2 * BY_VEC * P + BY_ACT * P <= 44800
        w_hi = at("w_hi", 40192, [P, 2, NP], F32R)
        w_lo = at("w_lo", 40768, [P, 2, NP], F32R)
        zero = at("zero", 41344, [P, 512])
        y_t = at("y_t", 0, [P, DC, NT])
        rows_ln2 = at("rows_ln2", 2432, [P, 2, D])

        taken = [0]

        def vec(n):
            taken[0] += n
            assert taken[0] <= 440
            return small[:, taken[0] - n:taken[0]]

        def col(name):
            a, n = COLS[name]
            return cols[:, a:a + n]

        s5v = [vec(16) for _ in range(22)]
        stats = vec(36)
        mv = vec(6)
        rstd = vec(6)
        lbv = vec(24)
        rms = vec(12)

        JOBS = [("xT", t, i) for t in range(3) for i in range(2)]
        JOBS += [("u", m) for m in range(4)] + [("f", m) for m in range(4)]
        JOBS += [("q", m) for m in range(4)]
        JOBS += [("w1T", b) for b in range(8)] + [("toep", b) for b in range(4)] + [("X", b) for b in range(6)]
        JOBS += [("v", t) for t in range(3)]
        LEVELS = [0, 1, 2, 4, 8, 16, 32, 64]

        def level_tiles(h):
            return [0, 1, 2] if h <= 8 else [0, 1]

        def tiles_before(h):
            return sum(len(level_tiles(k)) for k in LEVELS if 0 < k < h)

        BETWEEN = {h: job for h, job in zip(LEVELS, [("gate", t) for t in range(3)] + [("y", b) for b in range(3)])}
        for h in LEVELS:
            JOBS += [("att", h, t) for t in level_tiles(h)]
            if h in BETWEEN:
                JOBS += [BETWEEN[h]]
        JOBS += [("o", 0)] + [("kend", t) for t in range(3)]
        JOBS += [("S", 0), ("o", 1), ("S", 1), ("o", 2), ("S", 2)]
        JOBS += [("Sb", b) for b in range(NB)]
        JOBS += [("glu", m) for m in range(4)] + [("oT", t) for t in range(3)]
        for t in range(3):
            JOBS += [("mix", t, i) for i in range(2)]
            if t >= 1:
                JOBS += [("x1T", t - 1, i) for i in range(2)]
        JOBS += [("x1T", 2, i) for i in range(2)]
        for m in range(QB):
            JOBS += [("Q", m)]
            if m % 4 == 0 and m > 0:
                JOBS += [("sc", m // 4 - 1, t) for t in range(3)]
        JOBS += [("sc", 3, t) for t in range(3)]
        J = {name: n for n, name in enumerate(JOBS)}
        assert len(J) == len(JOBS)

        ps_full = sem("ps_full")
        ps_read = [sem(f"ps_read{i}") for i in range(8)]

        def bank_of(*name):
            return bank[J[name] % 8]

        def computed(eng, *name):
            if name[0] == "Q":
                eng.wait_ge(parts_used, 4 + 2 * (name[1] + 1))
            else:
                eng.wait_ge(ps_full, sum(other[0] != "Q" for other in JOBS[:J[name] + 1]))

        def readout(ins, *name):
            ins.then_inc(ps_read[J[name] % 8], 1)

        def evacuated(eng, *name):
            eng.wait_ge(ps_read[J[name] % 8], J[name] // 8 + 1)

        def x1_parts(t, i, a):
            t0, n = TILES[t]
            m = max(META - t0, 0)
            return (bank_of("x1T", t, i)[:, 0:4 * n].rearrange("p (c n) -> p c n", n=n)[:, :, m:n],
                    xw[:, a, 4 * i:4 * i + 4, t0 + m - META:t0 + n - META])

        x_in = [sem(f"x_in{t}") for t in range(3)]
        cols_sem = sem("cols_sem")
        rows_sem = sem("rows_sem")
        consts_sem = sem("consts_sem")
        masks_sem = sem("masks_sem")
        rowsv_sem = sem("rowsv_sem")
        w_loaded = [sem(f"w_loaded{i}") for i in range(2)]
        u4_moved = sem("u4_moved")
        z_moved = sem("z_moved")
        wglu_sem = sem("wglu_sem")
        keys_sem = sem("keys_sem")
        rows1_sem = sem("rows1_sem")
        s0_sem = sem("s0_sem")
        out_sem = sem("out_sem")
        uv_landed = [sem(f"uv_landed{i}") for i in range(4)]
        dch, ach, pch = sem("vector_chain"), sem("scalar_chain"), sem("gpsimd_chain")
        ln_var = sem("ln_var")
        ln_std = sem("ln_std")
        x0_ready = sem("x0_ready")
        dt_ready = sem("dt_ready")
        zr_ready = sem("zr_ready")
        mag_ready = sem("mag_ready")
        sin_arg = sem("sin_arg")
        sin_ready = sem("sin_ready")
        abar_ready = sem("abar_ready")
        lb_arg = sem("lb_arg")
        lb_exp = sem("lb_exp")
        w1_ready = sem("w1_ready")
        cpow_ready = sem("cpow_ready")
        rot_ready = sem("rot_ready")
        zeroed = sem("zeroed")
        f_pre = sem("f_pre")
        hin_ready = sem("hin_ready")
        q_decayed = sem("q_decayed")
        k_decayed = sem("k_decayed")
        suf_ready = sem("suf_ready")
        gate_s = sem("gate_s")
        gate_done = sem("gate_done")
        qm_ready = sem("qm_ready")
        vm_ready = sem("vm_ready")
        z_ready = sem("z_ready")
        s0_scaled = sem("s0_scaled")
        fins_ready = sem("fins_ready")
        ms_ready = sem("ms_ready")
        rms_ready = sem("rms_ready")
        og_ready = sem("og_ready")
        glu_s = sem("glu_s")
        x1_ready = sem("x1_ready")
        xw_ready = sem("xw_ready")
        tk_neg = sem("tk_neg")
        tk_exp = sem("tk_exp")
        idx_ready = sem("idx_ready")
        hi_ready = sem("hi_ready")
        lo_ready = sem("lo_ready")
        parts_used = sem("parts_used")
        gelu_done = sem("gelu_done")
        idxT_full = sem("idxT_full")
        idxT_ready = sem("idxT_ready")
        hot1_ready = sem("hot1_ready")
        hot2_ready = sem("hot2_ready")
        apart_ready = sem("apart_ready")
        gate_act = sem("gate_act")
        gate_pool = sem("gate_pool")
        hot_used = sem("hot_used")
        scaled_vec = sem("scaled_vec")
        factor_ready = sem("factor_ready")
        scaled_pool = sem("scaled_pool")
        whi_ready = sem("whi_ready")
        wlo_ready = sem("wlo_ready")
        zero_ready = sem("zero_ready")
        yT_ready = sem("yT_ready")
        yj_full = sem("yj_full")
        yj_read = sem("yj_read")
        rows2_sem = sem("rows2_sem")
        centred = sem("centred")
        scaled = sem("scaled")
        y_out_ready = sem("y_out_ready")
        y_last_ready = sem("y_last_ready")

        def chain(eng, s):
            count = [0]

            def link(ins):
                count[0] += 1
                ins.then_inc(s, 1)
                eng.wait_ge(s, count[0])
            return link

        def cmul(eng, link, out, x, a, tmp):
            eng.tensor_tensor(tmp[0], x[0], a[0], ALU.mult)
            eng.tensor_tensor(tmp[1], x[1], a[1], ALU.mult)
            eng.tensor_tensor(tmp[2], x[0], a[1], ALU.mult)
            link(eng.tensor_tensor(tmp[3], x[1], a[0], ALU.mult))
            eng.tensor_tensor(out[0], tmp[0], tmp[1], ALU.subtract)
            link(eng.tensor_tensor(out[1], tmp[2], tmp[3], ALU.add))

        def cmul_conj(eng, link, out, x, a, tmp):
            eng.tensor_tensor(tmp[0], x[0], a[0], ALU.mult)
            eng.tensor_tensor(tmp[1], x[1], a[1], ALU.mult)
            eng.tensor_tensor(tmp[2], x[1], a[0], ALU.mult)
            link(eng.tensor_tensor(tmp[3], x[0], a[1], ALU.mult))
            eng.tensor_tensor(out[0], tmp[0], tmp[1], ALU.add)
            link(eng.tensor_tensor(out[1], tmp[2], tmp[3], ALU.subtract))

        def wide(v, n):
            return v.unsqueeze(2).broadcast_to([P, NPAIR, n])

        masks = mask_words[:, :].bitcast(U8)

        def mask(h, t):
            k = [0, 1, 2, 4, 8, 16].index(h)
            if t < 2:
                m, w, n = masks[:, k * 128:(k + 1) * 128], 128, 128
            else:
                m, w, n = masks[:48, 768 + k * 48:768 + (k + 1) * 48], 48, 48
            return m.unsqueeze(1).broadcast_to([n, HEADS, w])

        w_groups = [(w_in, 2048), (w_in, 512), (w_in, 0), (w_in, 1024), (w_in, 1536),
                    (w_out, 0), (w_out, 512)]
        W_LAST = [("u", 3), ("f", 3), ("q", 3), ("v", 2), ("gate", 2)]
        W_GROUP = {"u": 0, "f": 1, "q": 2, "v": 3, "gate": 4}

        (dt_, zr, zi, mag, sn, cs, ar, ai, kk_, r_, den, nr, t1, t2, cr, ci, p2r, p2i, a4r, a4i,
         m4, absr) = s5v
        a_bar = (ar, ai)

        block = ctx.enter_context(nc.Block())

        @block.sync
        def _(sp):
            sp.dma_start(x_tok[0:META, 0, :], meta).then_inc(x_in[0], 16)
            sp.dma_start(x_tok[META:P, 0, :], x_prompt[0:112, :]).then_inc(x_in[0], 16)
            for i in range(2):
                sp.dma_start(rows_emb[:, i, :], rows_in[i, :].partition_broadcast(P)).then_inc(rows_sem, 16)
            sp.dma_start(x_tok[:, 1, :], x_prompt[112:240, :]).then_inc(x_in[1], 16)
            sp.dma_start(x_tok[0:T2P, 2, :], x_prompt[240:256, :]).then_inc(x_in[2], 16)
            sp.dma_start(x_tok[T2P:48, 2, :], x_sample).then_inc(x_in[2], 16)
            sp.dma_start(cols[:, :], cols_in).then_inc(cols_sem, 16)
            sp.dma_start(s5raw[:, :, :, :].rearrange("p a b c -> p (a b c)"), s5bc).then_inc(cols_sem, 16)
            sp.dma_start(ident[:, :], consts_in[:, 0:P]).then_inc(consts_sem, 16)
            sp.dma_start(iota[:, :], consts_in[:, P:2 * P]).then_inc(consts_sem, 16)
            sp.dma_start(lane[:, :], consts_in[:, 2 * P:2 * P + 9]).then_inc(consts_sem, 16)

            def load_w(n):
                if n >= 2:
                    computed(sp, *W_LAST[n - 2])
                w, c0 = w_groups[n]
                sp.dma_start(w_ring[:, n % 2, :, :],
                             w[:, c0:c0 + 512].rearrange("(c p) e -> p c e", p=P)).then_inc(w_loaded[n % 2], 16)

            load_w(0)
            sp.dma_start(mask_words[:, :], masks_in).then_inc(masks_sem, 16)
            load_w(1)
            sp.dma_start(rows_v[:, 0:2, :].rearrange("p a b -> p (a b)"),
                         rows_in[2, :].partition_broadcast(P)).then_inc(rowsv_sem, 16)
            sp.dma_start(rows_v[:, 2, :], rows_in[7, 0:DHG].partition_broadcast(P)).then_inc(rowsv_sem, 16)
            for m in range(4):
                evacuated(sp, "u", m)
            for j in range(SC):
                for q in range(4):
                    sp.dma_start(u4[32 * j:32 * j + 32, :, :].rearrange("p (m q) n -> p m q n", q=4)[:, :, q, :],
                                 u_chan[32 * q:32 * q + 32, :, j, :]).then_inc(u4_moved, 16)
            for n in range(2, 7):
                load_w(n)
            sp.wait_ge(gate_done, 3)
            sp.dma_start(wglu[:, :, :], w_glu.rearrange("(c p) e -> p c e", p=P)).then_inc(wglu_sem, 16)
            sp.wait_ge(hin_ready, 1)
            for b in range(NB):
                sp.dma_start(s_samp[:, b, :, :], state[b].rearrange("h k v -> k h v")).then_inc(s0_sem, 16)
            sp.wait_ge(z_ready, 3)
            for j in range(SC):
                for q in range(4):
                    sp.dma_start(z_t[32 * q:32 * q + 32, :, j, :],
                                 z4[32 * j:32 * j + 32, :, :].rearrange("p (m q) n -> p m q n", q=4)[:, :, q, :]
                                 ).then_inc(z_moved, 16)
            computed(sp, "y", 2)
            for i in range(2):
                sp.dma_start(rows_ln1[:, i, :], rows_in[3 + i, :].partition_broadcast(P)).then_inc(rows1_sem, 16)
            computed(sp, "Sb", NB - 1)
            sp.wait_ge(og_ready, 3)
            sp.wait_ge(vm_ready, 9)
            sp.dma_start(keysT[:, :, :], keys_t).then_inc(keys_sem, 16)
            sp.wait_ge(fins_ready, 1)
            sp.dma_start(ssm_out, fins[:, :, :, :].rearrange("p a b c -> p (a b c)")).then_inc(out_sem, 16)
            evacuated(sp, "S", 2)
            sp.dma_start(hg_prompt.rearrange("h k v -> k h v"), s_prompt[:, :, :]).then_inc(out_sem, 16)
            for b in range(NB):
                evacuated(sp, "Sb", b)
                sp.dma_start(hg_sample[b].rearrange("h k v -> k h v"), s_samp[:, b, :, :]).then_inc(out_sem, 16)

            computed(sp, "mix", 2, 1)
            sp.wait_ge(out_sem, 16 * 10)
            for s in range(4):
                sp.dma_start(raw[:, s, :], blocks[s]).then_inc(uv_landed[s], 16)

            def load_blocks(i, slots=range(4)):
                for s in slots:
                    sp.wait_ge(lo_ready, 8 * i + 2 * (s + 1))
                    sp.dma_start(raw[:, s, :], blocks[bass.ds(4 * i + (s + 4), 1)].squeeze(0)
                                 ).then_inc(uv_landed[s], 16)

            with sp.Fori(0, V_ROUND - 1, 1) as i:
                load_blocks(i)
            load_blocks(V_ROUND - 1, (0, 1))
            sp.wait_ge(zero_ready, 1)
            load_blocks(V_ROUND - 1, (2, 3))
            with sp.Fori(V_ROUND, ROUNDS - 1, 1) as i:
                load_blocks(i)
            sp.wait_ge(parts_used, 8 * ROUNDS + 4)
            for i in range(2):
                sp.dma_start(rows_ln2[:, i, :], rows_in[5 + i, :].partition_broadcast(P)).then_inc(rows2_sem, 16)
            sp.wait_ge(y_out_ready, 1)
            sp.dma_start(y_prompt[0:112, :], x_tok[META:P, 0, :]).then_inc(out_sem, 16)
            sp.wait_ge(y_out_ready, 2)
            sp.dma_start(y_prompt[112:240, :], x_tok[:, 1, :]).then_inc(out_sem, 16)
            sp.wait_ge(y_last_ready, 1)
            sp.dma_start(y_prompt[240:256, :], x_tok[0:T2P, 2, :]).then_inc(out_sem, 16)
            sp.dma_start(y_sample, x_tok[T2P:48, 2, :]).then_inc(out_sem, 16)
            sp.wait_ge(out_sem, 16 * 14)

        @block.tensor
        def _(pe):
            def begin(*name):
                n = J[name]
                if n >= 8:
                    pe.wait_ge(ps_read[n % 8], n // 8)
                return bank[n % 8]

            mm = nc.tensor.matmul

            def transposes(name, srcs):
                b = begin(*name)
                for k, (src, n) in enumerate(srcs):
                    last = nc.tensor.transpose(b[:, k * n:(k + 1) * n], src, ident[:n, :n])
                last.then_inc(ps_full, 1)

            def x_transposes(kind, t):
                t0, n = TILES[t]
                for i in range(2):
                    transposes((kind, t, i), [(x_tok[:n, t, (4 * i + c) * P:(4 * i + c + 1) * P], n)
                                              for c in range(4)])

            pe.wait_ge(consts_sem, 48)
            for t in range(3):
                pe.wait_ge(x0_ready, t + 1)
                x_transposes("xT", t)

            def weights(n):
                pe.wait_ge(w_loaded[n % 2], 16 * (n // 2 + 1))
                return w_ring[:, n % 2, :, :]

            def project(kind):
                w = weights(W_GROUP[kind])
                for m in range(4):
                    b = begin(kind, m)
                    for c in range(DC):
                        last = mm(b[:, 0:NT], w[:, c, m * P:(m + 1) * P], x_t[:, c, :],
                                  start=c == 0, stop=c == DC - 1)
                    last.then_inc(ps_full, 1)

            def project_tok(kind, t):
                w = weights(W_GROUP[kind])
                t0, n = TILES[t]
                b = begin(kind, t)
                for c in range(DC):
                    last = mm(b[:n, :], x_t[:, c, t0:t0 + n], w[:, c, :], start=c == 0, stop=c == DC - 1)
                last.then_inc(ps_full, 1)

            for t in range(3):
                for i in range(2):
                    evacuated(pe, "xT", t, i)
            project("u")
            project("f")
            project("q")

            pe.wait_ge(w1_ready, 1)
            w1f = w1[:, :, :, :, :, :].rearrange("p r a j g c -> p (r a) (j g c)")
            for b8 in range(8):
                transposes(("w1T", b8), [(w1f[:, 4 * b8 + k, :], P) for k in range(4)])
            pe.wait_ge(cpow_ready, 1)
            cpf = c_pow[:, :, :, :, :, :].rearrange("p r a t g c -> p r a (t g c)")
            for b4 in range(4):
                b = begin("toep", b4)
                for k in range(4):
                    pair = 4 * b4 + k
                    for i in range(SC):
                        for r in range(2):
                            last = mm(b[32 * i:32 * i + 32, k * P + 32 * i:(k + 1) * P],
                                      w1f[:, r * NPAIR + pair, 96:128], cpf[:, r, pair, 0:P - 32 * i],
                                      start=r == 0, stop=r == 1, tile_position=(0, 32 * i))
                last.then_inc(ps_full, 1)


            for j in range(8):
                evacuated(pe, "w1T", j)
            pe.wait_ge(u4_moved, 16 * 16)
            w1tf = w1_t[:, :, :, :].rearrange("p r a s -> p (r a) s")
            for b6 in range(6):
                b = begin("X", b6)
                units = range(6 * b6, min(6 * b6 + 6, 32))
                for k, un in enumerate(units):
                    last = mm(b[:, k * NCH:(k + 1) * NCH], w1tf[:, un, :], u4[:, un % NPAIR, :],
                              start=True, stop=True)
                last.then_inc(ps_full, 1)

            for t in range(3):
                project_tok("v", t)

            def levels(h):
                for t in level_tiles(h):
                    t0, n = TILES[t]
                    b = begin("att", h, t)
                    if h:
                        pe.wait_ge(q_decayed, tiles_before(h) + t + 1)
                        pe.wait_ge(k_decayed, tiles_before(h) + t + 1)
                    for hd in range(HEADS):
                        kk = k_dec if h else k_t
                        qq = q_dec if h else q_t
                        last = mm(b[:n, hd * P:hd * P + n], kk[:, hd, t0:t0 + n], qq[:, hd, t0:t0 + n],
                                  start=True, stop=True)
                    last.then_inc(ps_full, 1)

            for m in range(4):
                evacuated(pe, "q", m)
                evacuated(pe, "f", m)
            pe.wait_ge(f_pre, 4)

            def chunk_outputs(b3):
                for i in range(4):
                    evacuated(pe, "toep", i)
                pe.wait_ge(hin_ready, 1)
                b = begin("y", b3)
                for k, pair in enumerate(range(6 * b3, min(6 * b3 + 6, NPAIR))):
                    o = b[:, k * NCH:(k + 1) * NCH]
                    mm(o, toep[:, pair, :], u4[:, pair, :], start=True, stop=False)
                    for r in range(2):
                        last = mm(o, cpf[:, r, pair, 32:160], h_in[:, r, pair, 0:NCH], start=False, stop=r == 1)
                last.then_inc(ps_full, 1)

            for h in LEVELS:
                levels(h)
                if h in BETWEEN:
                    kind, k = BETWEEN[h]
                    if kind == "gate":
                        project_tok("gate", k)
                    else:
                        chunk_outputs(k)

            def k_ends():
                for t, (t0, n) in enumerate(TILES):
                    pe.wait_ge(k_decayed, tiles_before(P) + t + 1)
                    b = begin("kend", t)
                    for hd in range(HEADS):
                        last = nc.tensor.transpose(b[:n, hd * P:(hd + 1) * P], k_dec[:, hd, t0:t0 + n], ident[:, :])
                    last.then_inc(ps_full, 1)

            for t in range(3):
                evacuated(pe, "v", t)
            for h in LEVELS:
                for t in level_tiles(h):
                    evacuated(pe, "att", h, t)
            for t, (t0, n) in enumerate(TILES):
                b = begin("o", t)
                if t == 1:
                    evacuated(pe, "S", 0)
                    pe.wait_ge(q_decayed, tiles_before(P) + 1)
                if t == 2:
                    evacuated(pe, "S", 1)
                    pe.wait_ge(qm_ready, 1)
                    pe.wait_ge(s0_sem, 16 * NB)
                for hd in range(HEADS):
                    o = b[:n, hd * P:(hd + 1) * P]
                    last = mm(o, att[:n, t, hd, 0:n], v_tok[:n, t, hd * P:(hd + 1) * P], start=True, stop=t == 0)
                    if t == 1:
                        last = mm(o, q_dec[:, hd, t0:t0 + n], s_prompt[:, hd, :], start=False, stop=True)
                    if t == 2:
                        last = mm(o, q_mask[:, 0, hd, :], s_prompt[:, hd, :], start=False, stop=False)
                        for g in range(NB):
                            last = mm(o, q_mask[:, 1 + g, hd, :], s_samp[:, g, hd, :], start=False,
                                      stop=g == NB - 1)
                last.then_inc(ps_full, 1)
                if t == 0:
                    k_ends()
                if t == 2:
                    pe.wait_ge(vm_ready, 9)
                evacuated(pe, "kend", t)
                b = begin("S", t)
                for hd in range(HEADS):
                    vv = v_mask[:, 0, hd * P:(hd + 1) * P] if t == 2 else v_tok[:n, t, hd * P:(hd + 1) * P]
                    last = mm(b[:, hd * P:(hd + 1) * P], k_end[:n, t, hd, :], vv, start=True, stop=True)
                last.then_inc(ps_full, 1)
            for g in range(NB):
                b = begin("Sb", g)
                for hd in range(HEADS):
                    last = mm(b[:, hd * P:(hd + 1) * P], k_end[:48, 2, hd, :],
                              v_mask[:, 1 + g, hd * P:(hd + 1) * P], start=True, stop=True)
                last.then_inc(ps_full, 1)

            pe.wait_ge(z_moved, 16 * 16)
            pe.wait_ge(wglu_sem, 16)
            for m in range(4):
                b = begin("glu", m)
                for c in range(4):
                    last = mm(b[:, 0:NT], wglu[:, c, m * P:(m + 1) * P],
                              z_t[:, c, :, :].rearrange("p j n -> p (j n)"), start=c == 0, stop=c == 3)
                last.then_inc(ps_full, 1)
            for t, (t0, n) in enumerate(TILES):
                pe.wait_ge(og_ready, t + 1)
                transposes(("oT", t), [(o_tok[:n, t, hd * P:(hd + 1) * P], n) for hd in range(HEADS)])

            for t, (t0, n) in enumerate(TILES):
                evacuated(pe, "oT", t)
                if t == 0:
                    pe.wait_ge(glu_s, 4)
                for i in range(2):
                    w = weights(5 + i)
                    b = begin("mix", t, i)
                    for c in range(DC):
                        src = ohg_t[:, c, t0:t0 + n] if c < 4 else ossm_t[:, c - 4, t0:t0 + n]
                        last = mm(b[:n, :], src, w[:, c, :], start=c == 0, stop=c == DC - 1)
                    last.then_inc(ps_full, 1)
                if t >= 1:
                    pe.wait_ge(x1_ready, t)
                    x_transposes("x1T", t - 1)
            pe.sem_inc(parts_used, 4)
            pe.wait_ge(x1_ready, 3)
            x_transposes("x1T", 2)

            def block_product(b, half, low):
                for c in range(DC):
                    if c % 4 == 0:
                        pe.wait_ge(lo_ready, low(c // 4))
                    w = parts[:, (half + c // 4) % 4, :, (c % 4) * P:(c % 4 + 1) * P]
                    for (a, x) in ((0, 0), (0, 1), (1, 0)):
                        last = mm(b[:, 0:NP], w[:, a, :], xw[:, x, c, :],
                                  start=(c == 0 and (a, x) == (0, 0)), stop=(c == DC - 1 and a == 1))
                    if c % 4 == 3:
                        last.then_inc(parts_used, 1)

            for t in range(3):
                for i in range(2):
                    evacuated(pe, "x1T", t, i)

            def key_products(g):
                if g == 0:
                    pe.wait_ge(keys_sem, 16)
                for m in range(4):
                    evacuated(pe, "Q", 4 * g + m)
                for t, (t0, n) in enumerate(PTILES):
                    b = begin("sc", g, t)
                    for m in range(4):
                        last = mm(b[:n, m * P:(m + 1) * P], q_peer[:, 4 * g + m, t0:t0 + n],
                                  keysT[:, 4 * g + m, :], start=True, stop=True)
                    last.then_inc(ps_full, 1)

            for m in range(QB):
                block_product(begin("Q", m), 2 * m, lambda h: 2 * m + h + 1)
                if m % 4 == 0 and m > 0:
                    key_products(m // 4 - 1)
            key_products(3)

            for k in range(8):
                n = max(j for j in range(len(JOBS)) if j % 8 == k)
                pe.wait_ge(ps_read[k], n // 8 + 1)

            def u_blocks(i):
                for s in range(4):
                    pe.wait_ge(gelu_done, 4 * i + (s + 1))
                    block_product(bank[s], 2 * s, lambda h: 8 * i + (2 * s + h + 1))

            with pe.Fori(U_ROUND, U_ROUND + SPLIT // 4, 1) as i:
                u_blocks(i)
            for t, (t0, n) in enumerate(PTILES):
                pe.wait_ge(idx_ready, t + 1)
                for a in range(3):
                    last = nc.tensor.transpose(bank[5 + t][:, a * n:(a + 1) * n], idx_f[:n, t, a, :], ident[:n, :n])
                last.then_inc(idxT_full, 1)
            with pe.Fori(U_ROUND + SPLIT // 4, V_ROUND, 1) as i:
                u_blocks(i)
            pe.wait_ge(gelu_done, 4 * V_ROUND + 4)
            pe.sem_inc(hot_used, 16)
            with pe.Fori(0, NP // 16, 1) as i:
                for u in range(16):
                    turn, v = u // 8, u % 8
                    if u % 4 == 0:
                        pe.wait_ge(scaled_vec if v == 0 else factor_ready, 2 * i + (turn + 1))
                    if v == 0:
                        pe.wait_ge(hot1_ready, 2 * i + (turn + 1))
                    if v < BY_ACT:
                        pe.wait_ge(gate_act, 2 * BY_ACT * i + (BY_ACT * turn + v + 2))
                    else:
                        pe.wait_ge(gate_pool, 2 * i + (turn + 3))
                    mm(bank[1 + u // 4][:, (u % 4) * P:(u % 4 + 1) * P], hot1[:, u, :], hot_g[:, u, :],
                       start=True, stop=True).then_inc(hot_used, 1)

            pe.wait_ge(zero_ready, 1)
            pe.wait_ge(scaled_vec, 2 + NP // 8)
            pe.wait_ge(factor_ready, 2 + NP // 8)
            for k in range(8):
                mm(bank[k][:, 0:NP], zero[0:1, 0:P], zero[0:1, 0:NP], start=True, stop=False, skip_group_check=True)
            with pe.Fori(0, NK // 2, 1) as i:
                for s in range(2):
                    pe.wait_ge(wlo_ready, 2 * i + (s + 1))
                    for c in range(DC):
                        if c % 4 == 0:
                            pe.wait_ge(lo_ready, 4 * i + (V_HALF + 2 * s + c // 4 + 1))
                        for (a, w) in ((0, w_hi), (0, w_lo), (1, w_hi)):
                            vv = parts[:, 2 * s + c // 4, a, (c % 4) * P:(c % 4 + 1) * P]
                            last = mm(bank[c][:, 0:NP], vv, w[:, s, :], start=False, stop=False,
                                      skip_group_check=True)
                        if c % 4 == 3:
                            last.then_inc(parts_used, 1)
            pe.wait_ge(yT_ready, 1 + DC)
            for t, (t0, n) in enumerate(TILES):
                for i in range(2):
                    k = 2 * t + i
                    b = bank[k]
                    for c in range(4):
                        last = nc.tensor.transpose(b[:n, c * P:(c + 1) * P], y_t[:, 4 * i + c, t0:t0 + n],
                                                   ident[:, :])
                    last.then_inc(yj_full, 1)

        @block.scalar
        def _(act):
            link = chain(act, ach)
            A = nc.scalar.activation

            def deviation(k, t):
                n = TILES[t][1]
                act.wait_ge(ln_var, 3 * k + t + 1)
                A(rstd[:n, 3 + t:4 + t], rstd[:n, t:t + 1], ACT.Sqrt).then_inc(ln_std, 1)

            def high_part(i, q):
                s = q // 2
                if q % 2 == 0:
                    act.wait_ge(uv_landed[s % 4], 16 * i + 16 * (s // 4 + 1))
                act.wait_ge(parts_used, 8 * i + (q + 1))
                A(parts[:, q % 4, 0, :], raw[:, s % 4, (q % 2) * 512:(q % 2 + 1) * 512], ACT.Copy
                  ).then_inc(hi_ready, 1)

            deviation(0, 0)
            for t, (t0, n) in enumerate(TILES):
                if t < 2:
                    deviation(0, t + 1)
                for i in range(2):
                    computed(act, "xT", t, i)
                    readout(A(x_t[:, 4 * i:4 * i + 4, t0:t0 + n],
                              bank_of("xT", t, i)[:, 0:4 * n].rearrange("p (c n) -> p c n", n=n), ACT.Copy),
                            "xT", t, i)
            act.wait_ge(cols_sem, 32)
            A(dt_, col("ldt"), ACT.Exp).then_inc(dt_ready, 1)
            act.wait_ge(zr_ready, 1)
            A(mag, zr, ACT.Exp).then_inc(mag_ready, 1)
            act.wait_ge(lb_arg, 1)
            A(lbv[:, 0:8], lbv[:, 0:8], ACT.Exp).then_inc(lb_exp, 1)
            act.wait_ge(sin_arg, 1)
            A(sn, r_, ACT.Sin)
            A(cs, absr, ACT.Sin).then_inc(sin_ready, 1)

            for m in range(4):
                computed(act, "u", m)
                b = bank_of("u", m)
                bias = col("bu")[:, m:m + 1]
                A(u_chan[:, m, :, 0:NB], b[:, NPROMPT:NT].rearrange("p (n j) -> p j n", j=SC),
                  ACT.Identity, bias=bias)
                readout(A(u_chan[:, m, :, NB:NCH], b[:, 0:NPROMPT].rearrange("p (n j) -> p j n", j=SC),
                          ACT.Identity, bias=bias), "u", m)
            act.wait_ge(cpow_ready, 1)
            act.wait_ge(lb_arg, 2)
            for m in range(4):
                computed(act, "f", m)
                b = bank_of("f", m)
                A(f_t[:, m, :], b[:, 0:NT], ACT.Sigmoid, bias=col("bf")[:, m:m + 1])
                readout(A(k_t[:, m, :], b[:, 0:NT], ACT.Sigmoid, bias=lbv[:, 12 + m:13 + m], scale=-1.0), "f", m)
            for m in range(4):
                computed(act, "q", m)
                readout(A(q_t[:, m, :], bank_of("q", m)[:, 0:NT], ACT.Identity, bias=col("bq")[:, m:m + 1]), "q", m)
            for b8 in range(8):
                computed(act, "w1T", b8)
                readout(A(w1_t[:, :, :, :].rearrange("p r a s -> p (r a s)")[:, b8 * 512:(b8 + 1) * 512],
                          bank_of("w1T", b8)[:, :], ACT.Copy), "w1T", b8)
            act.wait_ge(zeroed, 3)
            for b4 in range(4):
                computed(act, "toep", b4)
                b = bank_of("toep", b4)[:, :].rearrange("p (k s) -> p k s", s=P)
                for i in range(SC):
                    last = A(toep[32 * i:32 * i + 32, 4 * b4:4 * b4 + 4, 32 * i:P],
                             b[32 * i:32 * i + 32, :, 32 * i:P], ACT.Copy)
                readout(last, "toep", b4)
            xf = x_s5[:, :, :, :].rearrange("p r a n -> p (r a n)")
            act.wait_ge(cpow_ready, 1)
            act.wait_ge(w1_ready, 1)
            for b6 in range(6):
                computed(act, "X", b6)
                n = min(6, 32 - 6 * b6) * NCH
                readout(A(xf[:, 6 * b6 * NCH:6 * b6 * NCH + n], bank_of("X", b6)[:, 0:n], ACT.Copy), "X", b6)
            for t, (t0, n) in enumerate(TILES):
                evacuated(act, "gate", t)
                A(gate_sig[:n, t, :], gate[:n, t, :], ACT.Sigmoid).then_inc(gate_s, 1)
            for b3 in range(3):
                evacuated(act, "y", b3)
                n = min(6, NPAIR - 6 * b3)
                A(z4[:, 6 * b3:6 * b3 + n, :], z4[:, 6 * b3:6 * b3 + n, :], ACT.Gelu_apprx_tanh).then_inc(z_ready, 1)
            evacuated(act, "v", 2)
            computed(act, "y", 2)
            for g in range(9):
                A(v_mask[:, g, :], v_tok[:48, 2, :], ACT.Copy, scale=lane[:48, g:g + 1]).then_inc(vm_ready, 1)
            act.wait_ge(fins_ready, 1)

            def read_output(t):
                n = TILES[t][1]
                computed(act, "o", t)
                readout(A(o_tok[:n, t, :], bank_of("o", t)[:n, :], ACT.Copy), "o", t)

            read_output(0)
            act.wait_ge(gate_done, 3)
            for t, (t0, n) in enumerate(TILES):
                computed(act, "kend", t)
                readout(A(k_end[:n, t, :, :], bank_of("kend", t)[:n, :].rearrange("p (h k) -> p h k", k=P),
                          ACT.Copy), "kend", t)
            read_output(1)
            read_output(2)
            act.wait_ge(ms_ready, 1)
            A(rms[:, :], rms[:, :], ACT.Sqrt).then_inc(rms_ready, 1)
            for m in range(4):
                computed(act, "glu", m)
                b = bank_of("glu", m)
                readout(A(du[:, 4 * m:4 * m + 4, :].rearrange("p a n -> p (a n)"), b[:, 0:NT], ACT.Sigmoid,
                          bias=col("bglu")[:, m:m + 1]), "glu", m)
            for t, (t0, n) in enumerate(TILES):
                computed(act, "oT", t)
                readout(A(ohg_t[:, :, t0:t0 + n], bank_of("oT", t)[:, 0:4 * n].rearrange("p (h n) -> p h n", n=n),
                          ACT.Copy), "oT", t)
            deviation(1, 0)
            for t, (t0, n) in enumerate(TILES):
                if t < 2:
                    deviation(1, t + 1)
                for i in range(2):
                    src, dst = x1_parts(t, i, 0)
                    computed(act, "x1T", t, i)
                    A(dst, src, ACT.Copy).then_inc(xw_ready, 1)
                if t == 1:
                    for q in range(4):
                        high_part(0, q)
            evacuated(act, "Sb", NB - 1)
            evacuated(act, "S", 2)

            def read_scores(g):
                for t, (t0, n) in enumerate(PTILES):
                    computed(act, "sc", g, t)
                    readout(A(scores[:n, t, 4 * g:4 * g + 4, :],
                              bank_of("sc", g, t)[:n, :].rearrange("p (m k) -> p m k", k=NK), ACT.Copy), "sc", g, t)

            for m in range(QB):
                high_part(m // 4, 2 * (m % 4) + 4)
                high_part(m // 4, 2 * (m % 4) + 5)
                computed(act, "Q", m)
                readout(A(q_peer[:, m, :], bank_of("Q", m)[:, 0:NP], ACT.Copy), "Q", m)
                if m % 4 == 0 and m > 0:
                    read_scores(m // 4 - 1)
            act.sem_inc(gelu_done, 4 + QB)

            def u_blocks(i):
                for s in range(4):
                    high_part(i, 2 * s + 4)
                    high_part(i, 2 * s + 5)
                    act.wait_ge(parts_used, 8 * i + (2 * s + 6))
                    A(store[:, bass.ds(4 * i + (s - QB), 1), :].squeeze(1), bank[s][:, 0:NP],
                      ACT.Gelu_apprx_tanh).then_inc(gelu_done, 1)

            read_scores(3)
            with act.Fori(U_ROUND, U_ROUND + SPLIT // 4 - 4, 1) as i:
                u_blocks(i)
            act.wait_ge(tk_neg, 1)
            A(tk_sc[:, :, :, :], tk_sc[:, :, :, :], ACT.Exp).then_inc(tk_exp, 1)
            with act.Fori(U_ROUND + SPLIT // 4 - 4, U_ROUND + SPLIT // 4, 1) as i:
                u_blocks(i)
            act.wait_ge(idxT_full, 3)
            with act.Fori(U_ROUND + SPLIT // 4, V_ROUND, 1) as i:
                u_blocks(i)
            act.wait_ge(idxT_ready, 1)
            act.sem_inc(gate_act, 1)
            act.sem_inc(factor_ready, 2)
            act.wait_ge(lo_ready, V_HALF + 4)

            def gates(i, turn):
                before = 2 * BY_ACT * i + BY_ACT * turn
                act.wait_ge(gate_act, before + 1)
                for v in range(BY_ACT):
                    A(apart[:, v, :], iota[:, :], ACT.Abs, scale=-1.0,
                      bias=idx_t[:, 1, bass.ds(16 * i + (8 * turn + v), 1)]).then_inc(apart_ready, 1)
                for v in range(BY_ACT):
                    act.wait_ge(apart_ready, before + (v + 1))
                    act.wait_ge(hot_used, 16 * i + (8 * turn + v + 1))
                    A(hot_g[:, 8 * turn + v, :], apart[:, v, :], ACT.Relu, scale=-2.0,
                      bias=idx_t[:, 2, bass.ds(16 * i + (8 * turn + v), 1)]).then_inc(gate_act, 1)

            def copy_factor(i, turn):
                act.wait_ge(hot_used, 16 * i + (16 + 8 * turn + 8))
                act.wait_ge(scaled_pool, 2 * i + (turn + 1))
                A(factor[:, turn, :], bank[2 + 2 * turn][:, :], ACT.Copy).then_inc(factor_ready, 1)

            gates(0, 0)
            with act.Fori(0, NP // 16 - 1, 1) as i:
                gates(i, 1)
                copy_factor(i, 0)
                gates(i + 1, 0)
                copy_factor(i, 1)
            gates(NP // 16 - 1, 1)
            copy_factor(NP // 16 - 1, 0)
            copy_factor(NP // 16 - 1, 1)
            act.wait_ge(zero_ready, 1)

            def w_high(i, s):
                act.wait_ge(parts_used, 8 * i + (V_HALF + 2 * s + 2))
                A(w_hi[:, s % 2, :], store[:, bass.ds(4 * i + s, 1), :].squeeze(1), ACT.Copy
                  ).then_inc(whi_ready, 1)

            w_high(0, 0)
            w_high(0, 1)
            with act.Fori(0, NK // 4 - 1, 1) as i:
                for s in range(2, 6):
                    high_part(i + V_ROUND, 2 * s)
                    high_part(i + V_ROUND, 2 * s + 1)
                    w_high(i, s)
            for s in range(2, 4):
                high_part(ROUNDS - 1, 2 * s)
                high_part(ROUNDS - 1, 2 * s + 1)
                w_high(NK // 4 - 1, s)
            act.wait_ge(parts_used, 8 * ROUNDS + 4)
            act.wait_ge(yT_ready, 1)
            for c in range(0, DC, 2):
                A(y_t[:, c, META:NT], bank[c][:, 0:NP], ACT.Copy).then_inc(yT_ready, 1)
            for t in range(3):
                deviation(2, t)
                if t < 2:
                    n = TILES[t][1]
                    act.wait_ge(centred, t + 1)
                    A(x_tok[:n, t, :], x_tok[:n, t, :], ACT.Copy, scale=rstd[:n, 3 + t:4 + t]).then_inc(scaled, 1)

        @block.vector
        def _(dve):
            link = chain(dve, dch)
            V = dve

            def layer_norm(t, rows, k, rows_landed, ready, shared=False):
                n = TILES[t][1]
                for i in range(2):
                    last = V.bn_stats(stats[:n, 12 * t + 6 * i:12 * t + 6 * i + 6],
                                      x_tok[:n, t, 512 * i:512 * (i + 1)])
                link(last)
                link(V.bn_aggr(mv[:n, 2 * t:2 * t + 2], stats[:n, 12 * t:12 * t + 12]))
                V.tensor_scalar(rstd[:n, t:t + 1], mv[:n, 2 * t + 1:2 * t + 2], LN_EPS, None,
                                ALU.add).then_inc(ln_var, 1)
                dve.wait_ge(rows_landed, 32)
                x = x_tok[:n, t, :]
                link(V.scalar_tensor_tensor(x, x, mv[:n, 2 * t:2 * t + 1], rows[:n, 0, :], ALU.subtract, ALU.mult))
                dve.wait_ge(ln_std, 3 * k + t + 1)
                if shared:
                    V.reciprocal(rstd[:n, 3 + t:4 + t], rstd[:n, 3 + t:4 + t]).then_inc(centred, 1)
                    return
                link(V.reciprocal(rstd[:n, 3 + t:4 + t], rstd[:n, 3 + t:4 + t]))
                V.scalar_tensor_tensor(x, x, rstd[:n, 3 + t:4 + t], rows[:n, 1, :], ALU.mult,
                                       ALU.add).then_inc(ready, 1)

            link(V.memset(rms[:, :], 1.0))
            for t in range(3):
                dve.wait_ge(x_in[t], 16 if t == 1 else 32)
                layer_norm(t, rows_emb, 0, rows_sem, x0_ready)

            dve.wait_ge(cols_sem, 32)
            dve.wait_ge(dt_ready, 1)
            V.tensor_tensor(zr, col("are"), dt_, ALU.mult).then_inc(zr_ready, 1)
            link(V.tensor_tensor(zi, col("aim"), dt_, ALU.mult))
            link(V.tensor_scalar(kk_, zi, 0.15915494309189535, ROUND, ALU.mult, ALU.add))
            link(V.tensor_scalar(kk_, kk_, ROUND, None, ALU.subtract))
            link(V.scalar_tensor_tensor(r_, kk_, -TWO_PI_HI, zi, ALU.mult, ALU.add))
            link(V.scalar_tensor_tensor(r_, kk_, -TWO_PI_MID, r_, ALU.mult, ALU.add))
            link(V.scalar_tensor_tensor(r_, kk_, -TWO_PI_LO, r_, ALU.mult, ALU.add))
            link(V.tensor_scalar(r_, r_, -PI_IN, PI_IN, ALU.max, ALU.min))
            link(V.tensor_scalar(t1, r_, -1.0, None, ALU.mult))
            link(V.tensor_tensor(t1, t1, r_, ALU.max))
            V.tensor_scalar(absr, t1, -1.0, 1.5707963267948966, ALU.mult, ALU.add).then_inc(sin_arg, 1)
            link(V.tensor_tensor(lbv[:, 20:24], col("lb0"), col("lb1"), ALU.max))
            V.tensor_tensor(lbv[:, 0:4], col("lb0"), lbv[:, 20:24], ALU.subtract)
            V.tensor_tensor(lbv[:, 4:8], col("lb1"), lbv[:, 20:24], ALU.subtract).then_inc(lb_arg, 1)
            V.tensor_tensor(den, col("are"), col("are"), ALU.mult)
            link(V.tensor_tensor(t2, col("aim"), col("aim"), ALU.mult))
            link(V.tensor_tensor(den, den, t2, ALU.add))
            link(V.reciprocal(den, den))
            dve.wait_ge(lb_exp, 1)
            link(V.tensor_tensor(lbv[:, 20:24], lbv[:, 0:4], lbv[:, 4:8], ALU.add))
            link(V.reciprocal(lbv[:, 20:24], lbv[:, 20:24]))
            V.tensor_tensor(lbv[:, 8:12], lbv[:, 0:4], lbv[:, 20:24], ALU.mult)
            link(V.tensor_scalar(lbv[:, 12:16], col("bf"), -1.0, None, ALU.mult))
            V.tensor_scalar(lbv[:, 16:20], lbv[:, 8:12], -1.0, 1.0, ALU.mult, ALU.add).then_inc(lb_arg, 1)
            dve.wait_ge(sin_ready, 1)
            dve.wait_ge(mag_ready, 1)
            V.tensor_tensor(ar, mag, cs, ALU.mult)
            V.tensor_tensor(ai, mag, sn, ALU.mult).then_inc(abar_ready, 1)
            dve.wait_ge(abar_ready, 1)
            link(V.tensor_scalar(nr, ar, -1.0, None, ALU.add))
            tiny = (t1, t2, cr, ci)
            cmul_conj(V, link, (p2r, p2i), (nr, ai), (col("are"), col("aim")), tiny)
            V.tensor_tensor(cr, p2r, den, ALU.mult)
            link(V.tensor_tensor(ci, p2i, den, ALU.mult))
            c4 = [cm[:, k, :].rearrange("p (a c) -> p a c", c=16) for k in range(4)]
            braw = [s5raw[:, r, :, :] for r in range(2)]
            cmul(V, link, (w1c[:, 0, :, 3, :], w1c[:, 1, :, 3, :]), braw, (wide(cr, 16), wide(ci, 16)), c4)
            for j in (2, 1, 0):
                cmul(V, link, (w1c[:, 0, :, j, :], w1c[:, 1, :, j, :]),
                     (w1c[:, 0, :, j + 1, :], w1c[:, 1, :, j + 1, :]), (wide(ar, 16), wide(ai, 16)), c4)
            dve.wait_ge(zeroed, 1)
            for g in range(2):
                h = slice(64 * g, 64 * g + 64)
                last = V.tensor_copy(w1[h, :, :, :, g, :].rearrange("p r a j c -> p (r a) j c"),
                                     w1c[h, :, :, :, :].rearrange("p r a j c -> p (r a) j c"))
            last.then_inc(w1_ready, 1)
            tiny = (t1, t2, nr, den)
            cmul(V, link, (p2r, p2i), a_bar, a_bar, tiny)
            cmul(V, link, (a4r, a4i), (p2r, p2i), (p2r, p2i), tiny)
            link(V.tensor_tensor(m4, mag, mag, ALU.mult))
            link(V.tensor_tensor(m4, m4, m4, ALU.mult))
            link(V.tensor_copy(decay[:, :, :], wide(m4, NCP)))
            link(V.memset(decay[:, :, 0:1], 0.0))

            dve.wait_ge(lb_arg, 2)
            for m in range(HEADS):
                evacuated(dve, "f", m)
                oml = lbv[:, 16 + m:17 + m]
                V.tensor_scalar(f_t[:, m, :], f_t[:, m, :], oml, lbv[:, 8 + m:9 + m], ALU.mult, ALU.add)
                V.tensor_scalar(k_t[:, m, :], k_t[:, m, :], oml, None, ALU.mult).then_inc(f_pre, 1)
            dve.wait_ge(f_pre, 4)
            V.tensor_copy(pre[:, :, :], f_t[:, :, :])
            link(V.memset(suf[:, :, :], 1.0))

            for b6 in range(6):
                evacuated(dve, "X", b6)
            dve.wait_ge(rot_ready, 1)
            computed(dve, "toep", 3)
            computed(dve, "X", 5)
            X = [x_s5[:, r, :, :] for r in range(2)]
            G = [g_s5[:, r, :, :] for r in range(2)]
            H = [h_in[:, r, :, :] for r in range(2)]
            R = [rot[:, r, :, :] for r in range(2)]
            T = [cm_scan[:, r, :, :] for r in range(2)]
            for r, (op, other) in enumerate(((ALU.add, 1), (ALU.subtract, 0))):
                V.tensor_tensor(T[0], X[r][:, :, NB:NCH], R[0], ALU.mult)
                link(V.tensor_tensor(T[1], X[other][:, :, NB:NCH], R[1], ALU.mult))
                link(V.tensor_tensor(G[r], T[0], T[1], op))
            df = decay[:, :, :].rearrange("p a n -> p (a n)")
            for r in range(2):
                gf = G[r].rearrange("p a n -> p (a n)")
                last = V.tensor_tensor_scan(gf, df, gf, 0.0, ALU.mult, ALU.add)
            link(last)
            h0 = col("h0").rearrange("p (r a b) -> p r a b", r=2, b=NB)
            f8 = [cm[:, k, 0:128].rearrange("p (a b) -> p a b", b=NB) for k in range(4)]
            cmul(V, link, (fins[:, 0, :, 0:NB], fins[:, 1, :, 0:NB]), (h0[:, 0], h0[:, 1]),
                 (wide(a4r, NB), wide(a4i, NB)), f8)
            for r in range(2):
                last = V.tensor_tensor(fins[:, r, :, 0:NB], fins[:, r, :, 0:NB], X[r][:, :, 0:NB], ALU.add)
            link(last)
            for r, (op, other) in enumerate(((ALU.subtract, 1), (ALU.add, 0))):
                V.tensor_tensor(T[0], G[r], R[0], ALU.mult)
                link(V.tensor_tensor(T[1], G[other], R[1], ALU.mult))
                V.tensor_tensor(H[r][:, :, NB + 1:NCH], T[0][:, :, 0:NCP - 1], T[1][:, :, 0:NCP - 1], op)
                V.tensor_tensor(fins[:, r, :, NB:NB + 1], T[0][:, :, NCP - 1:NCP], T[1][:, :, NCP - 1:NCP], op)
                V.tensor_copy(H[r][:, :, 0:NB], h0[:, r])
                link(V.memset(H[r][:, :, NB:NB + 1], 0.0))
            V.sem_inc(hin_ready, 1)
            V.sem_inc(fins_ready, 1)
            dve.wait_ge(u4_moved, 16 * 16)
            link(V.tensor_tensor(du[:, :, :], u4[:, :, :], wide(col("d"), NCH), ALU.mult))

            dve.wait_ge(rowsv_sem, 32)
            for t, (t0, n) in enumerate(TILES):
                computed(dve, "v", t)
                readout(V.tensor_tensor(v_tok[:n, t, :], bank_of("v", t)[:n, :], rows_v[:n, 0, :], ALU.add), "v", t)

            dve.wait_ge(zeroed, 4)
            dve.wait_ge(masks_sem, 16)

            def pick(h):
                for t in level_tiles(h):
                    n = TILES[t][1]
                    computed(dve, "att", h, t)
                    b = bank_of("att", h, t)[:, :].rearrange("p (h s) -> p h s", s=P)
                    if h <= 16:
                        last = V.copy_predicated(att[:n, t, :, 0:n], mask(h, t), b[:n, :, 0:n])
                    elif h == 32:
                        V.tensor_copy(att[0:32, t, :, 32:64], b[0:32, :, 32:64])
                        last = V.tensor_copy(att[64:96, t, :, 96:128], b[64:96, :, 96:128])
                    else:
                        last = V.tensor_copy(att[0:64, t, :, 64:128], b[0:64, :, 64:128])
                    readout(last, "att", h, t)

            def read_between(kind, k):
                b = bank_of(kind, k)
                computed(dve, kind, k)
                if kind == "gate":
                    n = TILES[k][1]
                    last = V.tensor_tensor(gate[:n, k, :], b[:n, :], rows_v[:n, 1, :], ALU.add)
                else:
                    n = min(6, NPAIR - 6 * k)
                    a = slice(6 * k, 6 * k + n)
                    last = V.tensor_tensor(z4[:, a, :], b[:, 0:n * NCH].rearrange("p (a n) -> p a n", n=NCH),
                                           du[:, a, :], ALU.add)
                readout(last, kind, k)

            for m in range(HEADS):
                evacuated(dve, "q", m)
            for lv, h in enumerate(LEVELS[1:]):
                for t in level_tiles(h):
                    t0, n = TILES[t]
                    if lv:
                        computed(dve, "att", LEVELS[lv], t)
                    V.tensor_tensor(q_dec[:, :, t0:t0 + n], q_t[:, :, t0:t0 + n], pre[:, :, t0:t0 + n],
                                    ALU.mult).then_inc(q_decayed, 1)
                pick(LEVELS[lv])
                lim = NT if h <= 2 else NPROMPT if h <= 8 else 2 * P
                pv = pre[:, :, 0:lim].rearrange("p h (b s k) -> p h b s k", s=2, k=h)
                sv = suf[:, :, 0:lim].rearrange("p h (b s k) -> p h b s k", s=2, k=h)
                shape = [P, HEADS, lim // (2 * h), h]
                done = tiles_before(h) + len(level_tiles(h))
                dve.wait_ge(q_decayed, done)
                dve.wait_ge(k_decayed, done)
                V.tensor_tensor(sv[:, :, :, 0, :], sv[:, :, :, 0, :],
                                pv[:, :, :, 1, h - 1:h].broadcast_to(shape), ALU.mult).then_inc(suf_ready, 1)
                dve.wait_ge(suf_ready, lv + 1)
                link(V.tensor_tensor(pv[:, :, :, 1, :], pv[:, :, :, 1, :],
                                     pv[:, :, :, 0, h - 1:h].broadcast_to(shape), ALU.mult))
                if LEVELS[lv] in BETWEEN:
                    read_between(*BETWEEN[LEVELS[lv]])
            for t in range(2):
                computed(dve, "att", LEVELS[-1], t)
            pick(LEVELS[-1])
            V.tensor_tensor(q_dec[:, :, :], q_t[:, :, :], pre[:, :, :], ALU.mult).then_inc(q_decayed, 1)

            computed(dve, "S", 0)
            readout(V.tensor_copy(s_prompt[:, :, :].rearrange("p h v -> p (h v)"), bank_of("S", 0)[:, :]), "S", 0)
            for t in (1, 2):
                computed(dve, "S", t)
                last_col = (2 * P if t == 1 else NPROMPT) - 1
                evacuated(dve, "S", t - 1)
                for hd in range(HEADS):
                    last = V.scalar_tensor_tensor(s_prompt[:, hd, :], s_prompt[:, hd, :],
                                                  pre[:, hd, last_col:last_col + 1],
                                                  bank_of("S", t)[:, hd * P:(hd + 1) * P], ALU.mult, ALU.add)
                readout(last, "S", t)
            for t, (t0, n) in enumerate(TILES):
                evacuated(dve, "o", t)
                link(V.tensor_tensor(o_sq[:n, :], o_tok[:n, t, :], o_tok[:n, t, :], ALU.mult))
                link(V.reduce_sum(rms[:n, 4 * t:4 * t + 4], o_sq[:n, :].rearrange("p (h v) -> p h v", v=P), AX))
            V.tensor_scalar(rms[:, :], rms[:, :], 1.0 / P, RMS_EPS, ALU.mult, ALU.add).then_inc(ms_ready, 1)
            dve.wait_ge(s0_scaled, 1)
            for g in range(NB):
                computed(dve, "Sb", g)
                sg = s_samp[:, g, :, :].rearrange("p h v -> p (h v)")
                readout(V.tensor_tensor(sg, sg, bank_of("Sb", g)[:, :], ALU.add), "Sb", g)
            dve.wait_ge(rms_ready, 1)
            dve.wait_ge(gate_done, 3)
            link(V.reciprocal(rms[:, :], rms[:, :]))
            for t, (t0, n) in enumerate(TILES):
                ot = o_tok[:n, t, :].rearrange("p (h v) -> p h v", v=P)
                link(V.tensor_tensor(ot, ot, rms[:n, 4 * t:4 * t + 4].unsqueeze(2).broadcast_to([n, HEADS, P]),
                                     ALU.mult))
                V.tensor_tensor(o_tok[:n, t, :], o_tok[:n, t, :], gate[:n, t, :], ALU.mult).then_inc(og_ready, 1)

            for m in range(4):
                evacuated(dve, "glu", m)
                sg = du[:, 4 * m:4 * m + 4, :]
                V.tensor_tensor(ossm_t[:, m, 0:NPROMPT].rearrange("p (n j) -> p j n", j=SC),
                                z_t[:, m, :, NB:NCH], sg[:, :, NB:NCH], ALU.mult)
                V.tensor_tensor(ossm_t[:, m, NPROMPT:NT].rearrange("p (n j) -> p j n", j=SC),
                                z_t[:, m, :, 0:NB], sg[:, :, 0:NB], ALU.mult).then_inc(glu_s, 1)


            def x1_low(t):
                for i in range(2):
                    src, dst = x1_parts(t, i, 1)
                    dve.wait_ge(xw_ready, 2 * t + i + 1)
                    readout(V.tensor_tensor(dst, src, x1_parts(t, i, 0)[1].bitcast(F32), ALU.subtract), "x1T", t, i)

            for t, (t0, n) in enumerate(TILES):
                for i in range(2):
                    computed(dve, "mix", t, i)
                    xx = x_tok[:n, t, 512 * i:512 * (i + 1)]
                    readout(V.scalar_tensor_tensor(xx, xx, ALPHA, bank_of("mix", t, i)[:n, :], ALU.mult, ALU.add),
                            "mix", t, i)
                for i in range(2):
                    evacuated(dve, "mix", t, i)
                layer_norm(t, rows_ln1, 1, rows1_sem, x1_ready)
                if t >= 1:
                    x1_low(t - 1)
            x1_low(2)

            link(V.memset(tk_sc[:, :, :, :], 0.0))

            def top16(n, srcs):
                for half in range(2):
                    k = slice(8 * half, 8 * half + 8)
                    for s, v, ix in srcs:
                        last = V.max(v[:, k], s)
                    link(last)
                    for s, v, ix in srcs:
                        last = V.max_index(ix[:, k], v[:, k], s)
                    if half == 0:
                        link(last)
                        for s, v, ix in srcs:
                            last = V.match_replace(s, v[:, k], s, LOWEST)
                    link(last)

            for g in range(4):
                for t, (t0, n) in enumerate(PTILES):
                    evacuated(dve, "sc", g, t)
                    top16(n, [(scores[:n, t, 4 * g + m, :], tk_val[:n, m, :], tk_idx[:n, m, :]) for m in range(4)])
                    v = tk_val[:n, :, :].rearrange("p (h c) k -> p h c k", c=2)
                    V.tensor_copy(tk_idxf[:n, :, :], tk_idx[:n, :, :])
                    link(V.tensor_tensor(tk_cand[:n, :, :, :],
                                         v[:, :, 0, :].unsqueeze(3).broadcast_to([n, 2, TOPK, TOPK]),
                                         v[:, :, 1, :].unsqueeze(2).broadcast_to([n, 2, TOPK, TOPK]), ALU.add))
                    top16(n, [(tk_cand[:n, h, :, :].rearrange("p a b -> p (a b)"), tk_sc[:n, t, 2 * g + h, :],
                               tk_ci[:n, h, :]) for h in range(2)])
                    V.tensor_scalar(tk_ab[:n, 0, :, :], tk_ci[:n, :, :], 4, None, ALU.logical_shift_right)
                    link(V.tensor_scalar(tk_ab[:n, 1, :, :], tk_ci[:n, :, :], 15, None, ALU.bitwise_and))
                    link(V.tensor_copy(tk_abf[:n, :, :, :], tk_ab[:n, :, :, :]))
                    keys_of = tk_idxf[:n, :, :].rearrange("p (h c) k -> p h c k", c=2)
                    for c in range(2):
                        e = tk_eq[:n, c, :, :, :].rearrange("p h k a -> p (h k) a")
                        last = V.tensor_tensor(
                            e, tk_abf[:n, c, :, :].rearrange("p h k -> p (h k)").unsqueeze(2).broadcast_to([n, 32, TOPK]),
                            iota[:n, 0:TOPK].unsqueeze(1).broadcast_to([n, 32, TOPK]), ALU.is_equal)
                    link(last)
                    for c in range(2):
                        e = tk_eq[:n, c, :, :, :]
                        last = V.tensor_tensor(e, e, keys_of[:, :, c, :].unsqueeze(2).broadcast_to([n, 2, TOPK, TOPK]),
                                               ALU.mult)
                    link(last)
                    for c in range(2):
                        link(V.reduce_sum(idx_f[:n, t, c, 32 * g:32 * g + 32],
                                          tk_eq[:n, c, :, :, :].rearrange("p h k a -> p (h k) a"), AX))
            scv = tk_sc[:, :, :, :].rearrange("p t h k -> p (t h) k")
            link(V.tensor_copy(tk_sum[:, :], scv[:, :, 0:1].squeeze(2)))
            V.tensor_tensor(scv, scv, tk_sum[:, :].unsqueeze(2).broadcast_to([P, 24, TOPK]),
                            ALU.subtract).then_inc(tk_neg, 1)
            dve.wait_ge(tk_exp, 1)
            link(V.reduce_sum(tk_sum[:, :], scv, AX))
            link(V.reciprocal(tk_sum[:, :], tk_sum[:, :]))
            for t in range(3):
                V.tensor_tensor(idx_f[:, t, 2, :].rearrange("p (h k) -> p h k", k=TOPK), tk_sc[:, t, :, :],
                                tk_sum[:, 8 * t:8 * t + 8].unsqueeze(2).broadcast_to([P, PH, TOPK]),
                                ALU.mult).then_inc(idx_ready, 1)

            dve.wait_ge(idxT_full, 3)
            dve.wait_ge(gelu_done, 4 * V_ROUND + 4)
            for t, (t0, n) in enumerate(PTILES):
                last = V.tensor_copy(idx_t[:, :, t0:t0 + n],
                                     bank[5 + t][:, 0:3 * n].rearrange("p (a n) -> p a n", n=n))
            link(last)
            V.sem_inc(idxT_ready, 1)

            V.sem_inc(scaled_vec, 2)

            def hots(i, turn):
                dve.wait_ge(hot_used, 16 * i + 8 * (turn + 1))
                V.tensor_tensor(hot1[:, 8 * turn:8 * turn + 8, :], iota[:, :].unsqueeze(1).broadcast_to([P, 8, P]),
                                idx_t[:, 0, bass.ds(16 * i + 8 * turn, 8)].unsqueeze(2).broadcast_to([P, 8, P]),
                                ALU.is_equal).then_inc(hot1_ready, 1)
                dve.wait_ge(gate_pool, 2 * i + (turn + 1))
                V.tensor_tensor(hot2[:, turn, :, :], iota[:, :].unsqueeze(1).broadcast_to([P, BY_VEC, P]),
                                idx_t[:, 1, bass.ds(16 * i + (8 * turn + BY_ACT), BY_VEC)].unsqueeze(2)
                                .broadcast_to([P, BY_VEC, P]), ALU.is_equal).then_inc(hot2_ready, 1)

            def scale_store(i, turn):
                dve.wait_ge(hot_used, 16 * i + (16 + 8 * turn + 4))
                st = store[:, :, bass.ds(16 * i + 8 * turn, 4)]
                V.tensor_tensor(st, st, bank[1 + 2 * turn][:, :].rearrange("p (t j) -> p j t", j=NK),
                                ALU.mult).then_inc(scaled_vec, 1)

            hots(0, 0)
            with V.Fori(0, NP // 16 - 1, 1) as i:
                hots(i, 1)
                scale_store(i, 0)
                hots(i + 1, 0)
                scale_store(i, 1)
            hots(NP // 16 - 1, 1)
            scale_store(NP // 16 - 1, 0)
            scale_store(NP // 16 - 1, 1)
            dve.wait_ge(scaled_vec, 2 + NP // 8)
            dve.wait_ge(scaled_pool, 2 + NP // 8)
            V.memset(zero[:, :], 0.0).then_inc(zero_ready, 1)

            with V.Fori(0, NK // 2, 1) as i:
                for s in range(2):
                    dve.wait_ge(whi_ready, 2 * i + (s + 1))
                    V.tensor_tensor(w_lo[:, s, :], store[:, bass.ds(2 * i + s, 1), :].squeeze(1),
                                    w_hi[:, s, :].bitcast(F32), ALU.subtract).then_inc(wlo_ready, 1)

            dve.wait_ge(parts_used, 8 * ROUNDS + 4)
            V.memset(y_t[:, :, 0:META], 0.0).then_inc(yT_ready, 1)
            for c in range(1, DC, 2):
                V.tensor_copy(y_t[:, c, META:NT], bank[c][:, 0:NP]).then_inc(yT_ready, 1)
            for t, (t0, n) in enumerate(TILES):
                for i in range(2):
                    k = 2 * t + i
                    dve.wait_ge(yj_full, k + 1)
                    xx = x_tok[:n, t, 512 * i:512 * (i + 1)]
                    V.scalar_tensor_tensor(xx, xx, ALPHA, bank[k][:n, :], ALU.mult, ALU.add).then_inc(yj_read, 1)
                dve.wait_ge(yj_read, 2 * (t + 1))
                layer_norm(t, rows_ln2, 2, rows2_sem, y_last_ready, shared=t < 2)

        @block.gpsimd
        def _(pool):
            link = chain(pool, pch)
            G = pool
            G.memset(w1[:, :, :, :, :, :].rearrange("p r a j g c -> p (r a j g c)"), 0.0).then_inc(zeroed, 1)
            G.memset(c_pow[:, :, :, :, :, :].rearrange("p r a t g c -> p (r a t g c)"), 0.0).then_inc(zeroed, 1)
            G.memset(toep[:, :, :].rearrange("p a s -> p (a s)"), 0.0).then_inc(zeroed, 1)
            pool.wait_ge(abar_ready, 1)
            pool.wait_ge(cols_sem, 32)
            p4 = [pool_tmp[:, k, :].rearrange("p (a c) -> p a c", c=16) for k in range(4)]
            G.tensor_copy(c_cmp[:, 0, :, 0, :], s5raw[:, 2, :, :])
            link(G.tensor_scalar(c_cmp[:, 1, :, 0, :], s5raw[:, 3, :, :], -1.0, None, ALU.mult))
            for t in range(4):
                cmul_conj(G, link, (c_cmp[:, 0, :, t + 1, :], c_cmp[:, 1, :, t + 1, :]),
                     (c_cmp[:, 0, :, t, :], c_cmp[:, 1, :, t, :]), (wide(ar, 16), wide(ai, 16)), p4)
            pool.wait_ge(zeroed, 2)
            for g in range(2):
                h = slice(64 * g, 64 * g + 64)
                for r in range(2):
                    last = G.tensor_copy(c_pow[h, r, :, :, g, :], c_cmp[h, r, :, :, :])
                if g == 0:
                    link(last)
            last.then_inc(cpow_ready, 1)
            pool.wait_ge(cpow_ready, 1)
            rp = [pool_tmp[:, 0, 224:240], pool_tmp[:, 1, 224:240]]
            rq = [pool_tmp[:, 2, 224:240], pool_tmp[:, 3, 224:240]]
            tiny = [pool_tmp[:, k, 240:256] for k in range(4)]
            cmul(G, link, rq, (cs, sn), (cs, sn), tiny)
            cmul(G, link, rp, rq, rq, tiny)
            G.memset(rot[:, 0, :, 0:1], 1.0)
            link(G.memset(rot[:, 1, :, 0:1], 0.0))
            size = 1
            while size < NCP:
                done = 0
                count = min(size, NCP - size)
                while done < count:
                    n = min(14, count - done)
                    src = slice(done, done + n)
                    dst = slice(size + done, size + done + n)
                    tm = [pool_tmp[:, k, 0:16 * n].rearrange("p (a n) -> p a n", n=n) for k in range(4)]
                    cmul(G, link, (rot[:, 0, :, dst], rot[:, 1, :, dst]), (rot[:, 0, :, src], rot[:, 1, :, src]),
                         (wide(rp[0], n), wide(rp[1], n)), tm)
                    done += n
                cmul(G, link, rq, rp, rp, tiny)
                rp, rq = rq, rp
                size *= 2
            G.sem_inc(rot_ready, 1)
            pool.wait_ge(w1_ready, 1)
            pool.wait_ge(hin_ready, 1)
            G.memset(att[:, :, :, :].rearrange("p t h s -> p (t h s)"), 0.0).then_inc(zeroed, 1)
            G.memset(q_mask[:, :, :, :].rearrange("p g h s -> p (g h s)"), 0.0).then_inc(zeroed, 1)
            pool.wait_ge(f_pre, 4)
            for lv, h in enumerate(LEVELS[1:]):
                if lv:
                    pool.wait_ge(suf_ready, lv)
                for t in level_tiles(h):
                    t0, n = TILES[t]
                    if lv:
                        computed(pool, "att", LEVELS[lv], t)
                    G.tensor_tensor(k_dec[:, :, t0:t0 + n], k_t[:, :, t0:t0 + n], suf[:, :, t0:t0 + n],
                                    ALU.mult).then_inc(k_decayed, 1)
                if h >= 16:
                    t = {16: 0, 32: 1, 64: 2}[h]
                    n = TILES[t][1]
                    pool.wait_ge(gate_s, t + 1)
                    link(G.tensor_tensor(gate[:n, t, :], gate[:n, t, :], gate_sig[:n, t, :], ALU.mult))
                    G.tensor_tensor(gate[:n, t, :], gate[:n, t, :], rows_v[:n, 2, :], ALU.mult).then_inc(gate_done, 1)
            pool.wait_ge(suf_ready, len(LEVELS) - 1)
            for t in range(2):
                computed(pool, "att", LEVELS[-1], t)
            for t0, n in TILES:
                G.tensor_tensor(k_dec[:, :, t0:t0 + n], k_t[:, :, t0:t0 + n], suf[:, :, t0:t0 + n],
                                ALU.mult).then_inc(k_decayed, 1)
            pool.wait_ge(zeroed, 5)
            pool.wait_ge(q_decayed, tiles_before(P) + 1)
            G.tensor_copy(q_mask[:, 0, :, 0:T2P], q_dec[:, :, 2 * P:NPROMPT])
            for b in range(NB):
                c = T2P + NS * b
                last = G.tensor_copy(q_mask[:, 1 + b, :, c:c + NS], q_dec[:, :, 2 * P + c:2 * P + c + NS])
            last.then_inc(qm_ready, 1)
            computed(pool, "o", 2)
            tot = pre[:, :, NPROMPT:NT].rearrange("p h (b j) -> p b h j", j=NS)[:, :, :, NS - 1:NS]
            for b in range(NB):
                last = G.tensor_tensor(s_samp[:, b, :, :], s_samp[:, b, :, :],
                                       tot[:, b, :, :].broadcast_to([P, HEADS, P]), ALU.mult)
            last.then_inc(s0_scaled, 1)
            def low_part(i, q):
                pool.wait_ge(hi_ready, 8 * i + (q + 1))
                G.tensor_tensor(parts[:, q % 4, 1, :], raw[:, q // 2 % 4, (q % 2) * 512:(q % 2 + 1) * 512],
                                parts[:, q % 4, 0, :].bitcast(F32), ALU.subtract).then_inc(lo_ready, 1)

            with pool.Fori(0, V_ROUND, 1) as i:
                for q in range(8):
                    low_part(i, q)
            for q in range(4):
                low_part(V_ROUND, q)
            pool.wait_ge(idxT_ready, 1)
            pool.wait_ge(lo_ready, V_HALF + 4)
            pool.sem_inc(gate_pool, 2)
            pool.sem_inc(scaled_pool, 2)

            def gates(i, turn):
                pool.wait_ge(hot2_ready, 2 * i + (turn + 1))
                pool.wait_ge(hot_used, 16 * i + 8 * (turn + 1))
                G.tensor_tensor(hot_g[:, 8 * turn + BY_ACT:8 * turn + 8, :], hot2[:, turn, :, :],
                                idx_t[:, 2, bass.ds(16 * i + (8 * turn + BY_ACT), BY_VEC)].unsqueeze(2)
                                .broadcast_to([P, BY_VEC, P]), ALU.mult).then_inc(gate_pool, 1)

            def scale_last(i, turn):
                pool.wait_ge(factor_ready, 2 * i + (turn + 3))
                st = store[:, :, bass.ds(16 * i + (8 * turn + 4), 4)]
                G.tensor_tensor(st, st, factor[:, turn, :].rearrange("p (t j) -> p j t", j=NK),
                                ALU.mult).then_inc(scaled_pool, 1)

            gates(0, 0)
            with pool.Fori(0, NP // 16 - 1, 1) as i:
                gates(i, 1)
                scale_last(i, 0)
                gates(i + 1, 0)
                scale_last(i, 1)
            gates(NP // 16 - 1, 1)
            scale_last(NP // 16 - 1, 0)
            scale_last(NP // 16 - 1, 1)
            with pool.Fori(V_ROUND, ROUNDS - 1, 1) as i:
                for q in range(4, 12):
                    low_part(i, q)
            for q in range(4, 8):
                low_part(ROUNDS - 1, q)
            pool.wait_ge(rows2_sem, 32)
            for t in range(2):
                n = TILES[t][1]
                pool.wait_ge(scaled, t + 1)
                G.tensor_tensor(x_tok[:n, t, :], x_tok[:n, t, :], rows_ln2[:n, 1, :], ALU.add).then_inc(y_out_ready, 1)


def kernel(x_prompt, x_sample, state_hgrn, state_ssm_re, state_ssm_im, meta_tokens, ln_emb_g, ln_emb_b,
           lb_logits, w_in, b_in, hg_norm_g, ssm_a_re, ssm_a_im, ssm_log_dt, ssm_b_re, ssm_b_im,
           ssm_c_re, ssm_c_im, ssm_d, w_glu, b_glu, w_out, ln1_g, ln1_b, peer_w_q, peer_keys,
           peer_u, peer_v, ln2_g, ln2_b):
    import numpy as np
    import concourse.bacc as bacc
    from concourse.bass_utils import run_bass_kernel_spmd

    def arr(a):
        return np.asarray(a)

    def by_chunk(v):
        return arr(v).reshape(-1, P).T

    def by_state(a):
        a = arr(a)
        a = a.reshape((NPAIR, 2, 64) + a.shape[2:])
        return np.moveaxis(a, 0, 2).reshape((P, NPAIR) + a.shape[3:])

    b_in0 = arr(b_in)[0]
    log_dt = np.repeat(arr(ssm_log_dt)[0][:, None], 64, axis=1)
    d_rows = np.tile(arr(ssm_d)[0].reshape(NPAIR, 32).T, (SC, 1))
    h0 = np.stack([by_state(np.moveaxis(arr(s)[0], 0, 2)) for s in (state_ssm_re, state_ssm_im)], axis=1)
    cols = np.concatenate([by_chunk(b_in0[0:512]), by_chunk(b_in0[512:1024]), by_chunk(b_in0[2048:2560]),
                           by_chunk(arr(b_glu)[0]), by_chunk(arr(lb_logits)[0]), by_chunk(arr(lb_logits)[1]),
                           by_state(arr(ssm_a_re)[0]), by_state(arr(ssm_a_im)[0]), by_state(log_dt), d_rows,
                           h0.reshape(P, -1)], axis=1)
    s5bc = np.stack([by_state(arr(ssm_b_re)[0]), by_state(arr(ssm_b_im)[0]),
                     by_state(np.swapaxes(arr(ssm_c_re)[0], 1, 2)), by_state(np.swapaxes(arr(ssm_c_im)[0], 1, 2))],
                    axis=1).reshape(P, -1)
    hg_row = np.concatenate([arr(hg_norm_g)[0], np.zeros(512, np.float32)])
    rows = np.stack([arr(ln_emb_g), arr(ln_emb_b), b_in0[1024:2048], arr(ln1_g)[0], arr(ln1_b)[0],
                     arr(ln2_g)[0], arr(ln2_b)[0], hg_row])
    s, t = np.meshgrid(np.arange(P), np.arange(P), indexing="ij")
    full = [s == t] + [(s // (2 * h) == t // (2 * h)) & (s % (2 * h) < h) & (t % (2 * h) >= h)
                       for h in (1, 2, 4, 8, 16)]
    last = [m & ((h < 4) | ((s < T2P) & (t < T2P))) for m, h in zip(full, (0, 1, 2, 4, 8))]
    masks = np.concatenate(full + [m[:, 0:48] for m in last], axis=1).astype(np.uint8)
    masks = np.ascontiguousarray(masks).view(np.uint32)
    group = np.where(np.arange(P) < T2P, 0, 1 + (np.arange(P) - T2P) // NS)
    consts = np.concatenate([np.eye(P), np.tile(np.arange(P), (P, 1)), group[:, None] == np.arange(9)[None, :]],
                            axis=1).astype(np.float32)
    arrays = {
        "x_prompt": arr(x_prompt)[0], "x_sample": arr(x_sample).reshape(NSAMP, D), "meta": arr(meta_tokens),
        "state": arr(state_hgrn)[0], "cols": cols, "s5bc": s5bc, "rows": rows, "masks": masks, "consts": consts,
        "w_in": arr(w_in)[0], "w_glu": arr(w_glu)[0], "w_out": arr(w_out)[0],
        "keys": arr(peer_keys)[0].reshape(2 * PH, NK, P).transpose(2, 0, 1),
        "blocks": np.concatenate([arr(peer_w_q)[0].reshape(DC, P, QB, P).transpose(2, 1, 0, 3).reshape(QB, P, D),
                              arr(peer_u)[0].reshape(NK, NK, DC, P).transpose(1, 3, 2, 0).reshape(NK, P, D),
                              arr(peer_v)[0].reshape(NK, NK, D).transpose(1, 0, 2)]),
    }
    arrays = {f"in_{k}": np.ascontiguousarray(a) for k, a in arrays.items()}
    outs = {"y_prompt": [SEQ, D], "y_sample": [NSAMP, D], "hg_prompt": [HEADS, P, P],
            "hg_sample": [NB, HEADS, P, P], "ssm": [P, 2 * NPAIR * 9]}
    nc = bacc.Bacc("TRN2", target_bir_lowering=False, num_devices=1)
    args = [nc.dram_tensor(k, a.shape, mybir.dt.from_np(a.dtype), kind="ExternalInput").ap()
            for k, a in arrays.items()]
    args += [nc.dram_tensor(f"out_{k}", sh, F32, kind="ExternalOutput").ap() for k, sh in outs.items()]
    trunk(nc, *args)
    r = run_bass_kernel_spmd(nc, [arrays], core_ids=[0]).results[0]
    ssm = np.asarray(r["out_ssm"]).reshape(2, 64, 2, NPAIR, 9).transpose(2, 4, 3, 0, 1).reshape(2, 9, 32, 64)
    return (np.asarray(r["out_y_prompt"]).reshape(1, SEQ, D), np.asarray(r["out_y_sample"]).reshape(NB, NS, D),
            np.asarray(r["out_hg_prompt"]).reshape(1, 1, HEADS, P, P), ssm[0, 8:9][None], ssm[1, 8:9][None],
            np.asarray(r["out_hg_sample"]).reshape(1, NB, HEADS, P, P), ssm[0, 0:8][None], ssm[1, 0:8][None])
```
